# Optimizing a Trainium2 kernel written in Bass

```python
import jax, jax.numpy as jnp
from jax import lax
import numpy as np

D_MODEL = 1024
BATCH = 1
SEQ = 512
DEPTH = 2

D_MIX = D_MODEL
MLA_HEADS = 4
MLA_NOPE = 128
MLA_ROPE = 64
MLA_V = 128
MLA_Q_RANK = 256
MLA_KV_RANK = 128
MLA_WIDTH = MLA_HEADS * MLA_V
ROPE_BASE = 10000.0
Q_BLOCK = 128
RWKV_WIDTH = D_MIX - MLA_WIDTH
RWKV_HEAD = 64
RWKV_HEADS = RWKV_WIDTH // RWKV_HEAD
DECAY_LORA = 64
AAA_LORA = 64
GATE_LORA = 128
GN_EPS = 64e-5
D_FF = 2816
CONV_W = 3
EPS = 1e-6
MLA_SIZES = (MLA_Q_RANK, MLA_KV_RANK, MLA_ROPE)
RWKV_SIZES = (RWKV_WIDTH, RWKV_WIDTH, RWKV_WIDTH, DECAY_LORA, DECAY_LORA, AAA_LORA, AAA_LORA, GATE_LORA)
MLA_IN = MLA_Q_RANK + MLA_KV_RANK + MLA_ROPE
RWKV_IN = 3 * RWKV_WIDTH + 2 * DECAY_LORA + 2 * AAA_LORA + GATE_LORA
D_IN = MLA_IN + RWKV_IN

kernel_name = 'hybrid_mla_rwkv7_convffn_adaln_encoder'

def rms_norm(x, gain=None, eps=EPS):
    xf = x.astype(jnp.float32)
    y = xf * lax.rsqrt(jnp.mean(xf * xf, axis=-1, keepdims=True) + eps)
    if gain is not None:
        y = y * gain.astype(jnp.float32)
    return y.astype(x.dtype)

def _split(z, sizes):
    offs = []
    acc = 0
    for s in sizes[:-1]:
        acc += s
        offs.append(acc)
    return jnp.split(z, offs, axis=-1)

def shift_prev(z):
    return jnp.pad(z, ((0, 0), (1, 0), (0, 0)))[:, :-1]

def shift_next(z):
    return jnp.pad(z, ((0, 0), (0, 1), (0, 0)))[:, 1:]

def centred_token_shift(z, mu):
    return z + mu[0] * (shift_prev(z) - z) + mu[1] * (shift_next(z) - z)

def rope_tables(pos):
    half = MLA_ROPE // 2
    inv_freq = ROPE_BASE ** (-jnp.arange(half, dtype=jnp.float32) / half)
    ang = pos.astype(jnp.float32)[..., None] * inv_freq
    return jnp.cos(ang), jnp.sin(ang)

def apply_rope(x, cos, sin):
    x1, x2 = jnp.split(x, 2, axis=-1)
    cos = cos.astype(x.dtype)
    sin = sin.astype(x.dtype)
    return jnp.concatenate([x1 * cos - x2 * sin, x2 * cos + x1 * sin], axis=-1)

def mla_group(q_lat, kv_lat, k_pe, positions, q_norm, w_uq, kv_norm, w_ukv, out_norm):
    B, S, _ = q_lat.shape
    H = MLA_HEADS
    q = (rms_norm(q_lat, q_norm) @ w_uq).reshape(B, S, H, MLA_NOPE + MLA_ROPE)
    q_nope, q_pe = q[..., :MLA_NOPE], q[..., MLA_NOPE:]
    kv = (rms_norm(kv_lat, kv_norm) @ w_ukv).reshape(B, S, H, MLA_NOPE + MLA_V)
    k_nope, v = kv[..., :MLA_NOPE], kv[..., MLA_NOPE:]
    cos, sin = rope_tables(positions)
    q_pe = apply_rope(q_pe, cos[:, :, None, :], sin[:, :, None, :])
    k_pe = apply_rope(k_pe, cos, sin)
    scale = (MLA_NOPE + MLA_ROPE) ** -0.5
    n_blk = S // Q_BLOCK
    qn_b = (q_nope * scale).reshape(B, n_blk, Q_BLOCK, H, MLA_NOPE).transpose(1, 0, 2, 3, 4)
    qp_b = (q_pe * scale).reshape(B, n_blk, Q_BLOCK, H, MLA_ROPE).transpose(1, 0, 2, 3, 4)

    def attend(blk):
        qn, qp = blk
        s = jnp.einsum('bqhd,bkhd->bhqk', qn, k_nope) + jnp.einsum('bqhr,bkr->bhqk', qp, k_pe)
        p = jax.nn.softmax(s.astype(jnp.float32), axis=-1).astype(v.dtype)
        return jnp.einsum('bhqk,bkhd->bqhd', p, v)

    o = lax.map(attend, (qn_b, qp_b))
    o = o.transpose(1, 0, 2, 3, 4).reshape(B, S, H * MLA_V)
    return rms_norm(o, out_norm)

def wkv7_scan(r, w, k, v, kk, a, reverse):
    B, S, H, N = r.shape
    xs = tuple(t.astype(jnp.float32).transpose(1, 0, 2, 3) for t in (r, w, k, v, kk, a))

    def step(state, inp):
        r_t, w_t, k_t, v_t, kk_t, a_t = inp
        sa = jnp.einsum('bhvk,bhk->bhv', state, -kk_t)
        state = (state * w_t[:, :, None, :]
                 + sa[..., None] * (kk_t * a_t)[:, :, None, :]
                 + v_t[..., None] * k_t[:, :, None, :])
        y = jnp.einsum('bhvk,bhk->bhv', state, r_t)
        return state, y

    state0 = jnp.zeros((B, H, N, N), jnp.float32)
    _, ys = lax.scan(step, state0, xs, reverse=reverse)
    return ys.transpose(1, 0, 2, 3)

def rwkv_decay(xw, w0, w2):
    wl = (w0 + jnp.tanh(xw) @ w2).astype(jnp.float32)
    wl = -jax.nn.softplus(-wl) - 0.5
    return jnp.exp(-jnp.exp(wl))

def rwkv7_group(r, k, v, xw_f, xw_b, xa_f, xa_b, xg, w0, w2, a0, a2, g2, k_k, k_a, r_k, gn_g, gn_b):
    B, S, W = r.shape
    H, N = RWKV_HEADS, RWKV_HEAD

    def heads(t):
        return t.reshape(B, S, H, N)

    g = jax.nn.sigmoid(xg) @ g2
    kk = heads(k * k_k).astype(jnp.float32)
    kk = kk * lax.rsqrt(jnp.sum(kk * kk, axis=-1, keepdims=True) + 1e-12)

    def direction(xw, xa, d, reverse):
        w = rwkv_decay(xw, w0[d], w2[d])
        a = jax.nn.sigmoid(a0[d] + xa @ a2[d])
        k_d = k * (1 + (a - 1) * k_a)
        y = wkv7_scan(heads(r), heads(w), heads(k_d), heads(v), kk, heads(a), reverse)
        return y, k_d

    y_f, k_f = direction(xw_f, xa_f, 0, False)
    y_b, k_b = direction(xw_b, xa_b, 1, True)
    y = y_f + y_b
    mu = jnp.mean(y, axis=-1, keepdims=True)
    var = jnp.mean(jnp.square(y - mu), axis=-1, keepdims=True)
    y = ((y - mu) * lax.rsqrt(var + GN_EPS)).reshape(B, S, W) * gn_g + gn_b
    k_bonus = 0.5 * (k_f + k_b)
    bonus = jnp.sum(heads(r * k_bonus) * r_k, axis=-1, keepdims=True) * heads(v)
    return (y.astype(r.dtype) + bonus.reshape(B, S, W)) * g

def conv_ffn(h, w_up, conv_w, conv_b, w_down):
    u = h @ w_up
    gate, val = u[..., :D_FF], u[..., D_FF:]
    gate = conv_w[0] * shift_prev(gate) + conv_w[1] * gate + conv_w[2] * shift_next(gate) + conv_b
    return (jax.nn.silu(gate) * val) @ w_down

def setup_inputs(seed: int = 0) -> dict:
    key = jax.random.key(seed)
    ks = jax.random.split(key, 28)
    f32 = jnp.float32
    L = DEPTH
    W = RWKV_WIDTH

    def nrm(k, shape, scale):
        return scale * jax.random.normal(k, shape, f32)

    x = nrm(ks[0], (BATCH, SEQ, D_MODEL), 1.0)
    c = nrm(ks[1], (BATCH, D_MODEL), 1.0)
    positions = (jnp.arange(SEQ, dtype=jnp.int32)[None, :]
                 + jax.random.randint(ks[2], (BATCH, 1), 0, 1024, dtype=jnp.int32))
    ada_w = nrm(ks[3], (L, D_MODEL, 6 * D_MODEL), 0.5 * D_MODEL ** -0.5)
    ada_b = nrm(ks[4], (L, 6 * D_MODEL), 0.02)
    w_in = nrm(ks[5], (L, D_MODEL, D_IN), D_MODEL ** -0.5)
    mla_q_norm = 1.0 + nrm(ks[6], (L, MLA_Q_RANK), 0.05)
    mla_w_uq = nrm(ks[7], (L, MLA_Q_RANK, MLA_HEADS * (MLA_NOPE + MLA_ROPE)), MLA_Q_RANK ** -0.5)
    mla_kv_norm = 1.0 + nrm(ks[8], (L, MLA_KV_RANK), 0.05)
    mla_w_ukv = nrm(ks[9], (L, MLA_KV_RANK, MLA_HEADS * (MLA_NOPE + MLA_V)), MLA_KV_RANK ** -0.5)
    mla_out_norm = 1.0 + nrm(ks[10], (L, MLA_WIDTH), 0.05)
    rwkv_mu = jax.random.uniform(ks[11], (L, 2, RWKV_IN), f32, 0.0, 0.5)
    rwkv_w0 = jax.random.uniform(ks[12], (L, 2, W), f32, -6.0, 1.0)
    rwkv_w2 = nrm(ks[13], (L, 2, DECAY_LORA, W), 0.5 * DECAY_LORA ** -0.5)
    rwkv_a0 = nrm(ks[14], (L, 2, W), 0.1)
    rwkv_a2 = nrm(ks[15], (L, 2, AAA_LORA, W), 0.5 * AAA_LORA ** -0.5)
    rwkv_g2 = nrm(ks[16], (L, GATE_LORA, W), GATE_LORA ** -0.5)
    rwkv_k_k = 0.85 + nrm(ks[17], (L, W), 0.05)
    rwkv_k_a = 1.0 + nrm(ks[18], (L, W), 0.05)
    rwkv_r_k = nrm(ks[19], (L, RWKV_HEADS, RWKV_HEAD), 0.1)
    rwkv_gn_g = 1.0 + nrm(ks[20], (L, W), 0.05)
    rwkv_gn_b = nrm(ks[21], (L, W), 0.02)
    w_out = nrm(ks[22], (L, D_MIX, D_MODEL), D_MIX ** -0.5)
    ffn_w_up = nrm(ks[23], (L, D_MODEL, 2 * D_FF), D_MODEL ** -0.5)
    ffn_conv_w = nrm(ks[24], (L, CONV_W, D_FF), CONV_W ** -0.5)
    ffn_conv_b = nrm(ks[25], (L, D_FF), 0.02)
    ffn_w_down = nrm(ks[26], (L, D_FF, D_MODEL), D_FF ** -0.5)
    final_norm = 1.0 + nrm(ks[27], (D_MODEL,), 0.05)
    return {'x': x, 'c': c, 'positions': positions, 'ada_w': ada_w, 'ada_b': ada_b, 'w_in': w_in,
            'mla_q_norm': mla_q_norm, 'mla_w_uq': mla_w_uq, 'mla_kv_norm': mla_kv_norm,
            'mla_w_ukv': mla_w_ukv, 'mla_out_norm': mla_out_norm, 'rwkv_mu': rwkv_mu,
            'rwkv_w0': rwkv_w0, 'rwkv_w2': rwkv_w2, 'rwkv_a0': rwkv_a0, 'rwkv_a2': rwkv_a2,
            'rwkv_g2': rwkv_g2, 'rwkv_k_k': rwkv_k_k, 'rwkv_k_a': rwkv_k_a, 'rwkv_r_k': rwkv_r_k,
            'rwkv_gn_g': rwkv_gn_g, 'rwkv_gn_b': rwkv_gn_b, 'w_out': w_out, 'ffn_w_up': ffn_w_up,
            'ffn_conv_w': ffn_conv_w, 'ffn_conv_b': ffn_conv_b, 'ffn_w_down': ffn_w_down,
            'final_norm': final_norm}

def reference(x, c, positions, ada_w, ada_b, w_in, mla_q_norm, mla_w_uq, mla_kv_norm, mla_w_ukv,
              mla_out_norm, rwkv_mu, rwkv_w0, rwkv_w2, rwkv_a0, rwkv_a2, rwkv_g2, rwkv_k_k,
              rwkv_k_a, rwkv_r_k, rwkv_gn_g, rwkv_gn_b, w_out, ffn_w_up, ffn_conv_w, ffn_conv_b,
              ffn_w_down, final_norm):
    c_act = jax.nn.silu(c)
    for l in range(DEPTH):
        mod = c_act @ ada_w[l] + ada_b[l]
        sh1, sc1, gt1, sh2, sc2, gt2 = [m[:, None, :] for m in jnp.split(mod, 6, axis=-1)]

        h = rms_norm(x) * (1 + sc1) + sh1
        z = h @ w_in[l]
        z_mla, z_rwkv = z[..., :MLA_IN], z[..., MLA_IN:]
        q_lat, kv_lat, k_pe = _split(z_mla, MLA_SIZES)
        z_rwkv = centred_token_shift(z_rwkv, rwkv_mu[l])
        r, k, v, xw_f, xw_b, xa_f, xa_b, xg = _split(z_rwkv, RWKV_SIZES)
        y_mla = mla_group(q_lat, kv_lat, k_pe, positions, mla_q_norm[l], mla_w_uq[l],
                          mla_kv_norm[l], mla_w_ukv[l], mla_out_norm[l])
        y_rwkv = rwkv7_group(r, k, v, xw_f, xw_b, xa_f, xa_b, xg, rwkv_w0[l], rwkv_w2[l],
                             rwkv_a0[l], rwkv_a2[l], rwkv_g2[l], rwkv_k_k[l], rwkv_k_a[l],
                             rwkv_r_k[l], rwkv_gn_g[l], rwkv_gn_b[l])
        x = x + gt1 * (jnp.concatenate([y_mla, y_rwkv], axis=-1) @ w_out[l])

        h = rms_norm(x) * (1 + sc2) + sh2
        x = x + gt2 * conv_ffn(h, ffn_w_up[l], ffn_conv_w[l], ffn_conv_b[l], ffn_w_down[l])
    return rms_norm(x, final_norm)


_drawn_inputs = setup_inputs


def setup_inputs(seed=0):
    import zlib

    import numpy as np

    out = dict(_drawn_inputs(seed))
    spreads = {}
    factors = {'mla_q_norm': 8.0,
     'mla_kv_norm': 3.175,
     'mla_out_norm': 3.697,
     'rwkv_w2': 7.017,
     'rwkv_a0': 8.0,
     'rwkv_k_k': 2.693,
     'rwkv_k_a': 2.76,
     'rwkv_gn_g': 7.852,
     'rwkv_gn_b': 8.0,
     'ffn_conv_b': 8.0}
    for name, (base, spread) in spreads.items():
        noise = np.random.default_rng([zlib.crc32(name.encode()), seed]).standard_normal(out[name].shape)
        drawn = base * np.exp(spread * noise) if base else spread * noise
        out[name] = __import__('jax').numpy.asarray(drawn.astype(out[name].dtype))
    for name, factor in factors.items():
        out[name] = (out[name] * factor).astype(out[name].dtype)
    return out
```

```python
import numpy as np

import concourse.bass as bass
from concourse import mybir
from contextlib import ExitStack

F32 = mybir.dt.float32
I32 = mybir.dt.int32
U8 = mybir.dt.uint8
ALU = mybir.AluOpType
ACT = mybir.ActivationFunctionType
AX = mybir.AxisListType

P = 128
DM, SEQ, DEPTH = 1024, 512, 2
KD = DM // P
HEADS, NOPE, ROPE, VD = 4, 128, 64, 128
QR, KVR = 256, 128
QB = KVR_B = 2
RW = 512
RB = RW // P
C = 128
NCH = SEQ // C
FF = 2816
NF = FF // P
EPS, GN_EPS, KK_EPS = 1e-6, 64e-5, 1e-12
DECAY = -float(np.exp(-0.5))
SCALE = (NOPE + ROPE) ** -0.5
NPROJ = 19
NTILE = NPROJ + KD
LEVELS = [1, 2, 4, 8, 16, 32, 64]

_SIZES = [("ada_b", 48), ("q_gain", 2), ("kv_gain", 1), ("out_gain", 4), ("mu0", 15), ("mu1", 15),
          ("w0", 8), ("a0", 8), ("k_k", 4), ("k_a", 4), ("r_k", 4), ("gn_g", 4), ("gn_b", 4),
          ("conv_w", 66), ("conv_b", NF)]
PRM, _n = {}, 0
for _name, _w in _SIZES:
    PRM[_name] = _n
    _n += _w
NPRM = _n
DRV = {"w0h": 0, "a0h": 8, "ka_h": 16, "ka_c": 20, "r_kh": 24, "mu_c": 28}
NDRV = 43
K_ID, K_ONE, K_BD, K_SWAP, K_GF, K_SCAN, K_FREQ, K_SIGN, K_EPS, K_GNEPS, K_KKEPS, K_GAIN = (
    0, 128, 256, 384, 512, 1024, 1536, 1537, 1538, 1539, 1540, 1541)
NCST = 1541 + KD


class Steps:

    def __init__(self, sem, names):
        self.sem, self.names, self.turn = sem, names, 0
        self.index = {n: i for i, n in enumerate(names)}
        assert len(self.index) == len(names)

    def one(self, name):
        assert self.names[self.turn % len(self.names)] == name, (name, self.names[self.turn % len(self.names)])
        self.turn += 1
        return 1

    def at(self, name, rnd):
        return (rnd + 1) * len(self.names) + (self.index[name] + 1)

    def before(self, name, rnd):
        return rnd * len(self.names) + (self.index[name] + 1)


def trunk(nc, x, c, pos, cst, lev, prm, tiles, up, down, ada, mlaw, lora, out):
    ctx = ExitStack()
    with ctx:
        def sb(name, cols, dt=F32):
            return ctx.enter_context(nc.sbuf_tensor(name, [P, cols], dt))

        def steps(name, names):
            return Steps(ctx.enter_context(nc.semaphore(name)), names)

        def sem(name):
            return ctx.enter_context(nc.semaphore(name))

        def view(t, off, *dims):
            n = int(np.prod(dims))
            ap = t[:, off:off + n]
            if len(dims) == 2:
                ap = ap.rearrange("p (a b) -> p a b", a=dims[0])
            if len(dims) == 3:
                ap = ap.rearrange("p (a b c) -> p a b c", a=dims[0], b=dims[1])
            if len(dims) == 4:
                ap = ap.rearrange("p (a b c d) -> p a b c d", a=dims[0], b=dims[1], c=dims[2])
            return ap

        X = sb("x_res", KD * SEQ)
        Y = sb("y_mix", KD * SEQ)
        CST = sb("constants", NCST)
        LEV = sb("level_masks", len(LEVELS) * 2 * P, U8)
        PR = sb("params", NPRM)
        DR = sb("derived", NDRV)
        TRIG = sb("cos_sin", 2 * SEQ)
        RING = sb("proj_weights", 3 * KD * P)
        SQ = sb("squares", 2 * SEQ)
        RS = sb("rstd", 2 * SEQ)
        MODR = sb("mod_raw", 48)
        MOD = sb("mod", 48)
        MIX = sb("mixer_inputs", NF * SEQ)
        WORK = sb("work", 21760)

        PS = [ctx.enter_context(nc.psum_tensor(f"bank{i}", [P, 512], F32)) for i in range(8)]

        xk = lambda k: X[:, k * SEQ:(k + 1) * SEQ]
        yk = lambda k: Y[:, k * SEQ:(k + 1) * SEQ]
        at = lambda t, b: t[:, bass.ds(b * SEQ, SEQ)]
        col = lambda t, i: t[:, bass.ds(i, 1)] if not isinstance(i, int) else t[:, i:i + 1]
        ident = CST[:, K_ID:K_ID + P]
        ones = CST[:, K_ONE:K_ONE + P]
        head_ones = CST[:, K_BD:K_BD + P]
        swap = CST[:, K_SWAP:K_SWAP + P]
        gmask = [CST[:, K_GF + 256 * d:K_GF + 256 * d + 256] for d in range(2)]
        scan_mask = CST[:, K_SCAN:K_SCAN + SEQ]
        k_eps, k_gneps, k_kkeps = CST[:, K_EPS:K_EPS + 1], CST[:, K_GNEPS:K_GNEPS + 1], CST[:, K_KKEPS:K_KKEPS + 1]

        def level_mask(s, d, transposed):
            j = 2 * LEVELS.index(s) + (d ^ int(transposed))
            return LEV[:, j * P:(j + 1) * P].unsqueeze(1).to_broadcast([P, NCH, P])

        cos, sin = TRIG[:, 0:SEQ], TRIG[:, SEQ:2 * SEQ]
        ring = [view(RING, s * KD * P, KD, P) for s in range(3)]
        sq = [SQ[:, i * SEQ:(i + 1) * SEQ] for i in range(2)]
        rs = [RS[:, i * SEQ:(i + 1) * SEQ] for i in range(2)]
        R0, K0, V0, KK0, XW, XA, XG, BON, GATE = 0, 4, 8, 12, 16, 17, 18, 19, 20
        mix = lambda i: MIX[:, i * SEQ:(i + 1) * SEQ]
        H = WORK[:, 0:KD * SEQ]
        hk = lambda k: H[:, k * SEQ:(k + 1) * SEQ]
        UPW = [view(WORK, 4096 + i * 2048, KD, 2, P) for i in range(2)]
        DNW = [view(WORK, 8192 + i * NF * P, NF, P) for i in range(2)]
        CV = [WORK[:, 13824 + i * SEQ:13824 + (i + 1) * SEQ] for i in range(2)]
        TH = [WORK[:, 14848 + i * SEQ:14848 + (i + 1) * SEQ] for i in range(2)]
        ADA = [WORK[:, 15872 + i * DM:15872 + (i + 1) * DM] for i in range(2)]
        LEV_IN = WORK[:, 0:len(LEVELS) * 2 * P]
        CACT = WORK[:, 20736:21760]
        RAW = view(WORK, 4096, 4, SEQ)
        LAT = view(WORK, 6144, 3, SEQ)
        MW = WORK[:, 7680:8960]
        KPE = WORK[:, 8960:9472]
        o = 9472
        QN = view(WORK, o, 2, SEQ)
        QPR = WORK[:, o + 1024:o + 1536]
        QPE = WORK[:, o + 1536:o + 2048]
        KN = view(WORK, o + 2048, 2, SEQ)
        VT_A = view(WORK, o + 3072, 4, 2 * P)
        PB = view(WORK, 0, 2, SEQ)
        PTb = [view(WORK, 17920 - 2048 * (1 - e) , 4, SEQ) for e in range(2)]
        KT1 = WORK[:, 0:512]
        KT2 = WORK[:, 512:1024]
        ZR = [view(WORK, 1024 * d, NCH, 2, C) for d in range(2)]
        BH = [WORK[:, 2048 + 512 * d:2560 + 512 * d] for d in range(2)]
        KH = [WORK[:, 3072 + 512 * d:3584 + 512 * d] for d in range(2)]
        TT = [view(WORK, 2048 + 512 * g, NCH, C) for g in range(4)]
        BT = [view(WORK, 4096 + 512 * d, NCH, P) for d in range(2)]
        KT = [view(WORK, 5120 + 512 * d, NCH, P) for d in range(2)]
        KDD = [WORK[:, 6144 + 512 * d:6656 + 512 * d] for d in range(2)]
        GB = [view(WORK, 7168 + 1024 * g, NCH, 2, C) for g in range(4)]
        GK = [view(WORK, 11264 + 1024 * g, NCH, 2, C) for g in range(4)]
        XX = [view(WORK, 15360 + 512 * g, NCH, C) for g in range(4)]
        XT = [view(WORK, 17408 + 512 * g, NCH, C) for g in range(4)]
        TMP = [WORK[:, 15360 + 512 * i:15872 + 512 * i] for i in range(6)]
        LW, AA, CW, PP, PI, BB = TMP
        VB = WORK[:, 19456:19968]
        VT = view(WORK, 19968, NCH, P)
        RHS = view(RS, 0, 2, P)
        SA = view(RS, 256, 2, P)
        SM = view(RS, 512, 2, P)
        SMD = view(RS, 768, 2, P)
        edges = sb("chunk_edges", 16)
        MID = [edges[:, 4 * d:4 * d + 4] for d in range(2)]
        EM = [edges[:, 8 + 4 * d:12 + 4 * d] for d in range(2)]

        def own(bank, d=None):
            ap = PS[bank][:, :].rearrange("p (d a v) -> p d a v", d=2, a=4)[:, :, 0::3, :]
            return ap if d is None else ap[:, d]
        lslot = view(sb("lora_weights", 3 * P), 0, 3, P)
        dots = sb("ada_dots", 2)
        nmax = sb("neg_max", 8)
        rsum = sb("row_sum", 8)

        x_in, const_in, prm_in = sem("x_in"), sem("const_in"), sem("prm_in")
        ring_in = [sem(f"ring_in{i}") for i in range(3)]
        up_in = [sem(f"up_in{i}") for i in range(2)]
        down_in = [sem(f"down_in{i}") for i in range(2)]
        ada_in = [sem(f"ada_in{i}") for i in range(2)]
        mla_in, lora_in, out_done = sem("mla_in"), sem("lora_in"), sem("out_done")
        cact_done, mod_kept = sem("cact_done"), sem("mod_kept")

        x_ready = steps("x_ready", [f"x{k}" for k in range(KD)])
        tile_done = steps("tile_done", [f"t{k}" for k in range(3)])
        ada_done = steps("ada_done", ["a0", "a1"])
        pro_v = steps("pro_v", [f"s{i}" for i in range(17)])
        pro_a = steps("pro_a", ["sin", "cos", "tanh"])
        nrm_a = steps("nrm_a", [f"sq{k}" for k in range(KD)] + ["ln", "rstd"] + [f"h{k}" for k in range(KD)])
        nrm_p = steps("nrm_p", [f"sum{k}" for k in range(KD)])
        nrm_v = steps("nrm_v", [f"h{k}" for k in range(KD)])
        lay_v = steps("lay_v", ["modA", "modA1", "w0h", "kah", "kac", "rkh", "mu01", "muc", "modB", "modB1"])
        in_a = steps("in_a", ["raw0", "raw1", "raw2", "raw3", "xw", "xa", "txw", "xg", "txg"])
        in_v = steps("in_v", ["xw1", "xw2", "xa1", "xa2", "xg1", "xg2", "sxg"])
        rkv_a = steps("rkv_a", ["r", "k", "v"])
        rkv_v = steps("rkv_v", ["r1", "r2", "k1", "k2", "v1", "v2"])
        sta_p = steps("sta_p", [f"s{i}" for i in range(7)] + ["perm"])
        sta_a = steps("sta_a", [f"sq{i}" for i in range(7)] + [f"{w}{i}" for i in range(6) for w in ("ln", "rs")])
        sta_v = steps("sta_v", [f"kk{b}" for b in range(4)] + ["kp1", "kp2", "kp3", "qn0", "qn1", "kvn"]
                      + [f"kkn{b}" for b in range(4)])
        att_a = ["qA", "qB", "qp"]
        att_v = ["kA", "kB", "v0", "v1", "rp1", "rp2", "rp3"]
        att_p = ["qA", "qB", "qp", "kA", "kB", "v0", "v1", "perm"]
        for i in range(9):
            if i < 8:
                att_p.append(f"sc{i}")
                att_v += [f"mx{i}", f"nm{i}"]
                att_a.append(f"ex{i}")
            if i >= 1:
                att_v.append(f"rc{i - 1}")
                att_p.append(f"tr{i - 1}")
                att_a.append(f"pt{i - 1}")
            if i in (4, 8):
                att_p.append(f"pv{i // 4 - 1}")
                att_v.append(f"o{i // 4 - 1}")
        att_a, att_v, att_p = steps("att_a", att_a), steps("att_v", att_v), steps("att_p", att_p)
        att_q = steps("att_q", [f"pn{i}" for i in range(8)])
        on_a = steps("on_a", [f"sq{i}" for i in range(4)] + ["ln", "rs"])
        on_p = steps("on_p", [f"s{i}" for i in range(4)])
        on_v = steps("on_v", [f"y{i}" for i in range(4)])
        G4 = range(4)
        rw_p = ["W0", "A0", "W1", "A1", "G", "VT"]
        for d in range(2):
            rw_p += [f"BT{d}", f"KT{d}"]
            for g in (2 * d, 2 * d + 1):
                rw_p += [f"{m}{g}{h}" for m in ("Gb", "Gk") for h in range(2)]
        rw_p += ["BON"] + [f"LT{g}" for g in G4]
        for s in LEVELS[1:]:
            rw_p += [f"T{s}{g}" for g in G4]
            for g in G4:
                rw_p += ([f"X{s}{g}"] if s < 64 else []) + [f"Z{s}{g}"]
        rw_a = ["W0", "A0", "Pi0", "Pp0", "Pe0", "em0", "VT", "BT0", "KT0",
                "W1", "A1", "gate", "Pi1", "Pp1", "Pe1", "em1", "BT1", "KT1"]
        for s in LEVELS[1:]:
            rw_a += [f"T{s}{g}" for g in G4]
        rw_v = []
        for d in range(2):
            rw_v += [f"{n}{d}" for n in ("lw", "cw", "mid", "cc", "ce", "em", "b1", "bh", "f")]
            for g in (2 * d, 2 * d + 1):
                rw_v += [f"{m}{g}{h}" for m in ("Gb", "Gk") for h in range(2)]
        rw_v += ["kbr", "bon"] + [f"{m}{g}" for g in G4 for m in ("X1", "Z1")]
        for s in LEVELS[1:]:
            for g in G4:
                rw_v += ([f"X{s}{g}"] if s < 64 else []) + [f"Z{s}{g}"]
        rw_q = ["vb"]
        for d in range(2):
            rw_q += [f"{n}{d}" for n in ("rt", "zt", "kd", "kt")]
        rw_q += ["kbs"] + [f"{m}{g}" for g in G4 for m in ("XI", "ZI")]
        for s in range(NCH):
            rw_p += [f"R{s}", f"SA{s}"] + ([f"S{s}"] if s < NCH - 1 else []) + [f"Y{s}"]
            rw_a += [f"R{s}"]
            rw_v += ([f"SD{s}"] if 0 < s < NCH - 1 else []) + [f"SA{s}"] + ([f"S{s}0", f"S{s}1"] if s < NCH - 1 else []) + ([f"SS{s}"] if 0 < s < NCH - 1 else [])
        rw_a += ["Yev"]
        rw_p += ["GM"]
        rw_v += ["yc"]
        rw_a += ["gsq"]
        rw_p += ["GV"]
        rw_a += ["gln", "grs"]
        rw_v += ["gn1", "gn2"]
        rw_q += ["gt"]
        rw_p, rw_a, rw_v, rw_q = steps("rw_p", rw_p), steps("rw_a", rw_a), steps("rw_v", rw_v), steps("rw_q", rw_q)
        up_p = steps("up_p", ["g0", "v0", "g1", "v1"])
        up_a = steps("up_a", ["cv0", "cv1", "th0", "th1"])
        up_v = steps("up_v", [f"{n}{q}" for q in range(2) for n in ("c1", "c2")] + [f"{n}{q}" for q in range(2) for n in ("s", "a")])
        down_p = steps("down_p", ["m0", "m1"])
        every = [x_ready, tile_done, ada_done, nrm_a, nrm_p, nrm_v, lay_v, in_a, in_v, rkv_a, rkv_v,
                 sta_p, sta_a, sta_v, att_a, att_v, att_p, att_q, on_a, on_p, on_v, rw_p, rw_a, rw_v, rw_q,
                 up_p, up_a, up_v, down_p, pro_v, pro_a]

        passed = {"pe": sem("pe_passed"), "dve": sem("dve_passed"), "pool": sem("pool_passed")}

        def settle(eng, name):
            eng.sem_inc(passed[name], 1)

        def credit(eng, mine):
            for s in mine:
                eng.sem_inc(s.sem, len(s.names))

        block = ctx.enter_context(nc.Block())

        @block.sync
        def _(sp):
            sp.dma_start(CST[:, :], cst).then_inc(const_in, 16)
            sp.dma_start(LEV_IN.bitcast(I32), lev).then_inc(const_in, 16)
            sp.dma_start(X[:, :].rearrange("p (k t) -> p k t", k=KD), x).then_inc(x_in, 16)
            for s in range(3):
                sp.dma_start(ring[s], tiles[s]).then_inc(ring_in[s], 16)

            def load_tile(l, t, last=False):
                sp.wait_ge(tile_done.sem, l * NTILE + t + (3 + 1))
                sp.dma_start(ring[t % 3], tiles[l * NTILE + t + 3]).then_inc(ring_in[t % 3], 16)

            with sp.Fori(0, DEPTH) as l:
                sp.wait_ge(up_v.sem, up_v.before("a1", l * (NF // 2)))
                sp.dma_start(PR[:, :], prm[l]).then_inc(prm_in, 16)
                for t in range(7):
                    load_tile(l, t)
                with sp.Fori(0, RB) as b:
                    for i in range(3):
                        sp.wait_ge(tile_done.sem, l * NTILE + b * 3 + (7 + i + 4))
                        sp.dma_start(ring[(7 + i) % 3], tiles[l * NTILE + b * 3 + (7 + i + 3)]).then_inc(
                            ring_in[(7 + i) % 3], 16)
                with sp.Fori(0, HEADS // 2) as hp:
                    sp.wait_ge(att_p.sem, att_p.before("v1", l * 2 + hp))
                    sp.wait_ge(rw_p.sem, rw_p.before("GV", l * RB))
                    sp.wait_ge(up_p.sem, up_p.before("v1", l * (NF // 2)))
                    sp.wait_ge(down_p.sem, down_p.before("m1", l * (KD // 2)))
                    sp.dma_start(MW, mlaw[l, hp]).then_inc(mla_in, 16)
                with sp.Fori(0, RB) as b:
                    sp.wait_ge(rw_p.sem, rw_p.before("G", l * RB + b))
                    sp.dma_start(lslot, lora[l, b]).then_inc(lora_in, 16)
                sp.wait_ge(rw_p.sem, rw_p.at("GV", l * RB + RB - 1))
                sp.wait_ge(rw_v.sem, rw_v.at("gn2", l * RB + RB - 1))
                for q in range(2):
                    sp.dma_start(UPW[q], up[l * NF + q]).then_inc(up_in[q], 16)
                for q in range(2):
                    sp.dma_start(DNW[q], down[l * KD + q]).then_inc(down_in[q], 16)
                for t in range(NPROJ, NTILE):
                    if t + 3 >= NTILE:
                        continue
                    load_tile(l, t)
                sp.wait_ge(tile_done.sem, (l + 1) * NTILE + 3)
                for s in range(3):
                    sp.dma_start(ring[s], tiles[(l + 1) * NTILE + s]).then_inc(ring_in[s], 16)
                with sp.Fori(0, NF // 2 - 1) as i:
                    for q in range(2):
                        sp.wait_ge(up_p.sem, up_p.at(f"v{q}", l * (NF // 2) + i))
                        sp.dma_start(UPW[q], up[l * NF + i * 2 + (2 + q)]).then_inc(up_in[q], 16)
                with sp.Fori(0, KD // 2 - 1) as i:
                    for q in range(2):
                        sp.wait_ge(down_p.sem, down_p.at(f"m{q}", l * (KD // 2) + i))
                        sp.dma_start(DNW[q], down[l * KD + i * 2 + (2 + q)]).then_inc(down_in[q], 16)
            for s in range(3):
                sp.wait_ge(ring_in[s], 16 * (DEPTH * NTILE // 3 + 1))
            for k in range(KD):
                sp.wait_ge(x_ready.sem, x_ready.at(f"x{k}", 2 * DEPTH + 1))
                sp.dma_start(out[k], xk(k)).then_inc(out_done, 16)
            sp.wait_ge(out_done, 16 * KD)

        @block.tensor
        def _(pe):
            credit(pe, [tile_done, nrm_p, sta_p, att_p, on_p, rw_p, up_p, down_p])
            mm = pe.matmul
            pe.wait_ge(const_in, 32)

            def norm_sums(n):
                for k in range(KD):
                    pe.wait_ge(nrm_a.sem, nrm_a.at(f"sq{k}", n))
                    mm(PS[7][:, :], ones, sq[k % 2], start=(k == 0), stop=(k == KD - 1)).then_inc(nrm_p.sem, nrm_p.one(f"sum{k}"))

            def project(l, t, bank, rhs, free):
                s = t % 3
                pe.wait_ge(ring_in[s], (l * (NTILE // 3) + (t // 3 + 1)) * 16)
                free()
                for k in range(KD):
                    if t == 0:
                        pe.wait_ge(nrm_a.sem, nrm_a.at(f"h{k}", 2 * l))
                    last = mm(PS[bank][:, :], ring[s][:, k, :], rhs(k), start=(k == 0), stop=(k == KD - 1))
                last.then_inc(tile_done.sem, tile_done.one(f"t{t % 3}"))

            with pe.Fori(0, DEPTH) as l:
                norm_sums(2 * l)
                for t in range(7):
                    project(l, t, t, hk, lambda: None)
                with pe.Fori(0, RB) as b:
                    for i in range(3):
                        t, bank = 7 + i, 4 + i
                        pe.wait_ge(ring_in[t % 3], (l * (NTILE // 3) + b + (t // 3 + 1)) * 16)
                        pe.wait_ge(in_v.sem, in_v.at(("xw2", "xa2", "xg2")[i], l))
                        pe.wait_ge(rkv_v.sem, rkv_v.before(("r2", "k2", "v2")[i], l * RB + b))
                        for k in range(KD):
                            last = mm(PS[bank][:, :], ring[t % 3][:, k, :], hk(k), start=(k == 0), stop=(k == KD - 1))
                        last.then_inc(tile_done.sem, tile_done.one(f"t{t % 3}"))
                pe.wait_ge(rkv_v.sem, rkv_v.at("v2", l * RB + RB - 1))
                for i in range(7):
                    pe.wait_ge(sta_a.sem, sta_a.at(f"sq{i}", l))
                    bank = (0, 0, 1, 2, 3, 4, 5)[i]
                    mm(PS[bank][:, :], ones if i < 3 else head_ones, sq[i % 2], start=(i != 1),
                       stop=(i != 0)).then_inc(sta_p.sem, sta_p.one(f"s{i}"))
                mm(PS[6][:, :], swap, RAW[:, 3, :], start=True, stop=True).then_inc(sta_p.sem, sta_p.one("perm"))
                with pe.Fori(0, HEADS // 2) as hp:
                    it = l * 2 + hp
                    wq = MW[:, 0:768].rearrange("p (c n) -> p c n", c=2)
                    wkv = MW[:, 768:1280]
                    pe.wait_ge(mla_in, (it + 1) * 16)
                    pe.wait_ge(sta_v.sem, sta_v.at("kkn3", l))
                    pe.wait_ge(sta_a.sem, sta_a.at("rs5", l))
                    pe.wait_ge(att_v.sem, att_v.before("o1", it))
                    pe.wait_ge(att_a.sem, att_a.before("pt7", it))
                    for j, name in enumerate(("qA", "qB", "qp")):
                        for k in range(2):
                            last = mm(PS[j][:, :], wq[:, k, j * P:(j + 1) * P], LAT[:, k, :], start=(k == 0), stop=(k == 1))
                        last.then_inc(att_p.sem, att_p.one(name))
                    for j, name in enumerate(("kA", "kB")):
                        mm(PS[3 + j][:, :], wkv[:, j * P:(j + 1) * P], LAT[:, 2, :], start=True,
                           stop=True).then_inc(att_p.sem, att_p.one(name))
                    for j in range(2):
                        for u in range(2):
                            tb = 2 * j + u
                            last = mm(PS[5 + j][:, u * 256:(u + 1) * 256], LAT[:, 2, tb * P:(tb + 1) * P], wkv[:, 256:512],
                                      start=True, stop=True)
                        last.then_inc(att_p.sem, att_p.one(f"v{j}"))
                    pe.wait_ge(att_a.sem, att_a.at("qp", it))
                    mm(PS[7][:, :], swap, QPR, start=True, stop=True).then_inc(att_p.sem, att_p.one("perm"))
                    pe.wait_ge(att_v.sem, att_v.at("rp3", it))
                    pe.wait_ge(att_a.sem, att_a.at("qB", it))
                    for i in range(9):
                        if i < 8:
                            e, qb = divmod(i, 4)
                            rows = slice(64 * e, 64 * e + 64)
                            if i >= 2:
                                pe.wait_ge(att_a.sem, att_a.at(f"ex{i - 2}", it))
                            mm(PS[i % 2][:, :], QN[:, e, qb * P:(qb + 1) * P], KN[:, e, :], start=True, stop=False)
                            mm(PS[i % 2][:, :], QPE[rows, qb * P:(qb + 1) * P], KPE[rows, :], start=False,
                               stop=True).then_inc(att_p.sem, att_p.one(f"sc{i}"))
                        if i >= 1:
                            j = i - 1
                            pe.wait_ge(att_q.sem, att_q.at(f"pn{j}", it))
                            if j >= 2:
                                pe.wait_ge(att_a.sem, att_a.at(f"pt{j - 2}", it))
                            for kb in range(4):
                                last = pe.transpose(PS[2 + j % 2][:, kb * P:(kb + 1) * P], PB[:, j % 2, kb * P:(kb + 1) * P], ident)
                            last.then_inc(att_p.sem, att_p.one(f"tr{j}"))
                        if i in (4, 8):
                            e = i // 4 - 1
                            pe.wait_ge(att_a.sem, att_a.at(f"pt{4 * e + 3}", it))
                            for kb in range(4):
                                last = mm(PS[4 + e][:, :], VT_A[:, kb, e * P:(e + 1) * P], PTb[e][:, kb, :],
                                          start=(kb == 0), stop=(kb == 3))
                            last.then_inc(att_p.sem, att_p.one(f"pv{e}"))
                for i in range(4):
                    pe.wait_ge(on_a.sem, on_a.at(f"sq{i}", l))
                    mm(PS[6][:, :], ones, sq[i % 2], start=(i == 0), stop=(i == 3)).then_inc(on_p.sem, on_p.one(f"s{i}"))
                with pe.Fori(0, RB) as b:
                    it = l * RB + b
                    A, V, Q = (lambda n: pe.wait_ge(rw_a.sem, rw_a.at(n, it))), (lambda n: pe.wait_ge(rw_v.sem, rw_v.at(n, it))), (
                        lambda n: pe.wait_ge(rw_q.sem, rw_q.at(n, it)))

                    def done(ins, name):
                        ins.then_inc(rw_p.sem, rw_p.one(name))

                    pe.wait_ge(lora_in, (it + 1) * 16)
                    pe.wait_ge(on_a.sem, on_a.at("rs", l))
                    pe.wait_ge(rw_a.sem, rw_a.before("grs", it))
                    pe.wait_ge(rw_v.sem, rw_v.before("gn2", it))
                    for d in range(2):
                        rows = slice(64 * d, 64 * d + 64)
                        done(mm(PS[2 * d][:, :], lslot[rows, 0, :], mix(XW)[rows, :], start=True, stop=True), f"W{d}")
                        done(mm(PS[2 * d + 1][:, :], lslot[rows, 1, :], mix(XA)[rows, :], start=True, stop=True), f"A{d}")
                    done(mm(PS[4][:, :], lslot[:, 2, :], mix(XG), start=True, stop=True), "G")
                    Q("vb")
                    for c4 in range(NCH):
                        last = pe.transpose(PS[5][:, c4 * P:(c4 + 1) * P], VB[:, c4 * P:(c4 + 1) * P], ident)
                    done(last, "VT")
                    for d in range(2):
                        V(f"bh{d}")
                        A("VT" if d == 0 else "BT0")
                        for c4 in range(NCH):
                            last = pe.transpose(PS[5][:, c4 * P:(c4 + 1) * P], BH[d][:, c4 * P:(c4 + 1) * P], ident)
                        done(last, f"BT{d}")
                        Q(f"kt{d}")
                        if d:
                            A("KT0")
                        for c4 in range(NCH):
                            last = pe.transpose(PS[6][:, c4 * P:(c4 + 1) * P], KH[d][:, c4 * P:(c4 + 1) * P], ident)
                        done(last, f"KT{d}")
                        A(f"A{d}")
                        if d == 0:
                            A("A1")
                        for g in (2 * d, 2 * d + 1):
                            rows = slice(64 * (g % 2), 64 * (g % 2) + 64)
                            for m, src in enumerate((BH[d], KH[d])):
                                for h in range(2):
                                    bank = 2 * m + h
                                    if g:
                                        V(f"{('Gb', 'Gk')[m]}{g - 1}{h}")
                                    for c4 in (2 * h, 2 * h + 1):
                                        last = mm(PS[bank][:, (c4 % 2) * 256:(c4 % 2) * 256 + 256],
                                                  src[rows, c4 * P:(c4 + 1) * P], ZR[d][rows, c4, :, :], start=True, stop=True)
                                    done(last, f"{('Gb', 'Gk')[m]}{g}{h}")
                    V("kbr")
                    done(mm(PS[7][:, :], head_ones, LW, start=True, stop=True), "BON")
                    V("bon")
                    V("Gk31")
                    A("gate")
                    A("KT1")
                    for g in G4:
                        for c4 in range(NCH):
                            last = pe.transpose(PS[2 * g + 1][:, c4 * P:(c4 + 1) * P], GB[g][:, c4, 0, :], ident)
                        done(last, f"LT{g}")
                    for j, s in enumerate(LEVELS[1:]):
                        for g in G4:
                            V(f"Z{LEVELS[j]}{g}")
                            for c4 in range(NCH):
                                last = mm(PS[2 * g][:, c4 * P:(c4 + 1) * P], GB[g][:, c4, 0, :], XX[g][:, c4, :], start=True, stop=True)
                            done(last, f"T{s}{g}")
                        for g in G4:
                            A(f"T{s}{g}")
                            if s < 64:
                                for c4 in range(NCH):
                                    last = mm(PS[2 * g + 1][:, c4 * P:(c4 + 1) * P], XT[g][:, c4, :], TT[g][:, c4, :], start=True, stop=True)
                                done(last, f"X{s}{g}")
                            for c4 in range(NCH):
                                last = mm(PS[2 * g][:, c4 * P:(c4 + 1) * P], TT[g][:, c4, :], XT[g][:, c4, :], start=True, stop=True)
                            done(last, f"Z{s}{g}")
                    V("Z643")
                    for s in range(NCH):
                        ch = (s, NCH - 1 - s)
                        rb = 0 if s % 2 == 0 else 4
                        for g in G4:
                            d = g // 2
                            last = mm(PS[rb][:, g * P:(g + 1) * P], GK[g][:, ch[d], 0, :], VT[:, ch[d], :],
                                      start=(g == 0), stop=(s == 0), skip_group_check=True)
                        if s:
                            V("S01" if s == 1 else f"SS{s - 1}")
                            for d in range(2):
                                last = mm(own(rb, d), ZR[d][:, ch[d], 0, :], SM[:, d, :], start=False, stop=True, skip_group_check=True)
                        done(last, f"R{s}")
                        for g in G4:
                            d, e = divmod(g, 2)
                            mm(PS[3][64 * e:64 * e + 64, ch[d] * P:(ch[d] + 1) * P], VT[:, ch[d], e * 64:(e + 1) * 64],
                               GK[g][:, ch[d], 1, :], start=(s == 0 and d == 0), stop=False, skip_group_check=True)
                        if s:
                            for d in range(2):
                                mm(PS[3][:, ch[d] * P:(ch[d] + 1) * P], SM[:, d, :], ZR[d][:, ch[d], 1, :], start=False, stop=False,
                                   skip_group_check=True)
                        A(f"R{s}")
                        if s:
                            V(f"SA{s - 1}")
                        for g in G4:
                            last = mm(PS[1][:, g * P:(g + 1) * P], XT[g][:, ch[g // 2], :], RHS[:, g // 2, :], start=True, stop=True)
                        done(last, f"SA{s}")
                        V(f"SA{s}")
                        if s < NCH - 1:
                            for d in range(2):
                                so = PS[2][:, d * P:(d + 1) * P]
                                mm(so, KT[d][:, ch[d], :], VT[:, ch[d], :], start=True, stop=False)
                                last = mm(so, BT[d][:, ch[d], :], SA[:, d, :], start=False, stop=True)
                            done(last, f"S{s}")
                        for g in G4:
                            d, e = divmod(g, 2)
                            last = mm(PS[3][64 * e:64 * e + 64, ch[d] * P:(ch[d] + 1) * P], SA[:, d, e * 64:(e + 1) * 64],
                                      GB[g][:, ch[d], 1, :], start=False, stop=(s == NCH - 1), skip_group_check=True)
                        done(last, f"Y{s}")
                    A("Yev")
                    done(mm(PS[5][:, :], head_ones, PP, start=True, stop=True), "GM")
                    A("gsq")
                    done(mm(PS[6][:, :], head_ones, sq[0], start=True, stop=True), "GV")
                pe.wait_ge(rw_q.sem, rw_q.at("gt", l * RB + RB - 1))
                pe.wait_ge(rw_v.sem, rw_v.at("gn2", l * RB + RB - 1))
                for m in range(KD):
                    t = NPROJ + m

                    def free():
                        if m >= 4:
                            pe.wait_ge(x_ready.sem, x_ready.at(f"x{m - 4}", 2 * l + 1))
                    project(l, t, m % 4, yk, free)
                norm_sums(2 * l + 1)
                pe.wait_ge(nrm_a.sem, nrm_a.at(f"h{KD - 1}", 2 * l + 1))
                settle(pe, "pe")
                with pe.Fori(0, NF // 2) as i:
                    it = l * (NF // 2) + i
                    for q in range(2):
                        pe.wait_ge(up_in[q], (it + 1) * 16)
                        pe.wait_ge(up_v.sem, up_v.before(f"a{q}", it))
                        for half in range(2):
                            for k in range(KD):
                                last = mm(PS[2 * q + half][:, :], UPW[q][:, k, half, :], hk(k), start=(k == 0), stop=(k == KD - 1))
                            last.then_inc(up_p.sem, up_p.one(f"{'gv'[half]}{q}"))
                pe.wait_ge(up_v.sem, up_v.at("a1", (l + 1) * (NF // 2) - 1))
                settle(pe, "pe")
                with pe.Fori(0, KD // 2) as i:
                    it = l * (KD // 2) + i
                    for q in range(2):
                        pe.wait_ge(down_in[q], (it + 1) * 16)
                        pe.wait_ge(x_ready.sem, (l * 2 + 2) * KD + i * 2 + (q + KD - 1))
                        for j in range(NF):
                            last = mm(PS[4 + q][:, :], DNW[q][:, j, :], mix(j), start=(j == 0), stop=(j == NF - 1))
                        last.then_inc(down_p.sem, down_p.one(f"m{q}"))
            norm_sums(2 * DEPTH)

        @block.scalar
        def _(act):
            credit(act, [pro_a, nrm_a, in_a, rkv_a, sta_a, att_a, on_a, rw_a, up_a])
            F = act.activation
            act.wait_ge(const_in, 32)
            act.wait_ge(pro_v.sem, pro_v.at("s16", 0))
            F(sin, sin, ACT.Sin).then_inc(pro_a.sem, pro_a.one("sin"))
            F(cos, cos, ACT.Sin).then_inc(pro_a.sem, pro_a.one("cos"))
            F(ADA[0], CACT, ACT.Tanh, scale=0.5).then_inc(pro_a.sem, pro_a.one("tanh"))
            act.wait_ge(x_in, 16)

            def norm(n, h=True):
                for k in range(KD):
                    act.wait_ge(x_ready.sem, x_ready.at(f"x{k}", n))
                    if k >= 2:
                        act.wait_ge(nrm_p.sem, nrm_p.at(f"sum{k - 2}", n))
                    F(sq[k % 2], xk(k), ACT.Square).then_inc(nrm_a.sem, nrm_a.one(f"sq{k}"))
                act.wait_ge(nrm_p.sem, nrm_p.at(f"sum{KD - 1}", n))
                F(rs[0], PS[7][:, :], ACT.Ln, bias=k_eps, scale=1.0 / DM).then_inc(nrm_a.sem, nrm_a.one("ln"))
                act.wait_ge(nrm_a.sem, nrm_a.at("ln", n))
                F(rs[1], rs[0], ACT.Exp, scale=-0.5).then_inc(nrm_a.sem, nrm_a.one("rstd"))
                if h is False:
                    return
                for k in range(KD):
                    act.wait_ge(nrm_v.sem, nrm_v.at(f"h{k}", n))
                    F(hk(k), hk(k), ACT.Identity, bias=MOD[:, h + k:h + k + 1]).then_inc(nrm_a.sem, nrm_a.one(f"h{k}"))

            def scaled(bank, dst, j):
                return F(dst, PS[bank][:, :], ACT.Identity, scale=col(DR, DRV["mu_c"] + j))

            with act.Fori(0, DEPTH) as l:
                act.wait_ge(lay_v.sem, lay_v.at("muc", l))
                norm(2 * l, 0)
                for j in range(4):
                    act.wait_ge(tile_done.sem, l * NTILE + (j + 1 + 3))
                    F(RAW[:, j, :], PS[j][:, :], ACT.Identity).then_inc(in_a.sem, in_a.one(f"raw{j}"))
                for j, name in enumerate(("xw", "xa", "xg")):
                    act.wait_ge(tile_done.sem, l * NTILE + (4 + j + 1 + 3))
                    scaled(4 + j, mix((XW, XA, XG)[j]), j).then_inc(in_a.sem, in_a.one(name))
                    if j == 1:
                        act.wait_ge(in_v.sem, in_v.at("xw2", l))
                        F(mix(XW), mix(XW), ACT.Tanh).then_inc(in_a.sem, in_a.one("txw"))
                    if j == 2:
                        act.wait_ge(in_v.sem, in_v.at("xg2", l))
                        F(mix(XG), mix(XG), ACT.Tanh, scale=0.5).then_inc(in_a.sem, in_a.one("txg"))
                with act.Fori(0, RB) as b:
                    for i, name in enumerate("rkv"):
                        act.wait_ge(tile_done.sem, l * NTILE + b * 3 + (7 + i + 1 + 3))
                        scaled(4 + i, MIX[:, bass.ds(b * SEQ + 4 * i * SEQ, SEQ)], b * 3 + (3 + i)).then_inc(rkv_a.sem, rkv_a.one(name))
                for i in range(7):
                    if i >= 2:
                        act.wait_ge(sta_p.sem, sta_p.at(f"s{i - 2}", l))
                    if i < 3:
                        if i == 0:
                            act.wait_ge(in_a.sem, in_a.at("txg", l))
                        src = RAW[:, i, :]
                    else:
                        act.wait_ge(sta_v.sem, sta_v.at(f"kk{i - 3}", l))
                        src = mix(KK0 + i - 3)
                    F(sq[i % 2], src, ACT.Square).then_inc(sta_a.sem, sta_a.one(f"sq{i}"))
                for i in range(6):
                    act.wait_ge(sta_p.sem, sta_p.at(f"s{i + 1}", l))
                    if i:
                        act.wait_ge(sta_a.sem, sta_a.at(f"rs{i - 1}", l))
                    F(rs[0], PS[i][:, :], ACT.Ln, bias=k_eps if i < 2 else k_kkeps,
                      scale=(1.0 / QR, 1.0 / KVR, 1, 1, 1, 1)[i]).then_inc(sta_a.sem, sta_a.one(f"ln{i}"))
                    act.wait_ge(sta_a.sem, sta_a.at(f"ln{i}", l))
                    if i:
                        act.wait_ge(sta_v.sem, sta_v.at(("", "qn1", "kvn", "kkn0", "kkn1", "kkn2")[i], l))
                    F(rs[1], rs[0], ACT.Exp, scale=-0.5).then_inc(sta_a.sem, sta_a.one(f"rs{i}"))
                with act.Fori(0, HEADS // 2) as hp:
                    it = l * 2 + hp
                    act.wait_ge(att_p.sem, att_p.before("pv1", it))
                    for j, (name, dst) in enumerate((("qA", QN[:, 0, :]), ("qB", QN[:, 1, :]), ("qp", QPR))):
                        act.wait_ge(att_p.sem, att_p.at(name, it))
                        F(dst, PS[j][:, :], ACT.Identity, scale=SCALE).then_inc(att_a.sem, att_a.one(name))
                    for i in range(9):
                        if i < 8:
                            act.wait_ge(att_v.sem, att_v.at(f"nm{i}", it))
                            if i >= 2:
                                act.wait_ge(att_p.sem, att_p.at(f"tr{i - 2}", it))
                            F(PB[:, i % 2, :], PS[i % 2][:, :], ACT.Exp, bias=nmax[:, i:i + 1],
                              accum_out=rsum[:, i:i + 1]).then_inc(att_a.sem, att_a.one(f"ex{i}"))
                        if i >= 1:
                            j = i - 1
                            e, qb = divmod(j, 4)
                            act.wait_ge(att_p.sem, att_p.at(f"tr{j}", it))
                            F(PTb[e][:, :, qb * P:(qb + 1) * P], PS[2 + j % 2][:, :].rearrange("p (a b) -> p a b", a=4),
                              ACT.Identity).then_inc(att_a.sem, att_a.one(f"pt{j}"))
                for i in range(4):
                    act.wait_ge(att_v.sem, att_v.at("o1", l * 2 + 1))
                    if i >= 2:
                        act.wait_ge(on_p.sem, on_p.at(f"s{i - 2}", l))
                    F(sq[i % 2], yk(i), ACT.Square).then_inc(on_a.sem, on_a.one(f"sq{i}"))
                act.wait_ge(on_p.sem, on_p.at("s3", l))
                F(rs[0], PS[6][:, :], ACT.Ln, bias=k_eps, scale=1.0 / (HEADS * VD)).then_inc(on_a.sem, on_a.one("ln"))
                act.wait_ge(on_a.sem, on_a.at("ln", l))
                F(rs[1], rs[0], ACT.Exp, scale=-0.5).then_inc(on_a.sem, on_a.one("rs"))
                with act.Fori(0, RB) as b:
                    it = l * RB + b
                    PEw = lambda n: act.wait_ge(rw_p.sem, rw_p.at(n, it))
                    V = lambda n: act.wait_ge(rw_v.sem, rw_v.at(n, it))
                    Q = lambda n: act.wait_ge(rw_q.sem, rw_q.at(n, it))
                    A = lambda n: act.wait_ge(rw_a.sem, rw_a.at(n, it))

                    def done(ins, name):
                        ins.then_inc(rw_a.sem, rw_a.one(name))

                    act.wait_ge(rw_p.sem, rw_p.before("GV", it))
                    act.wait_ge(rw_v.sem, rw_v.before("gn2", it))
                    act.wait_ge(rw_q.sem, rw_q.before("gt", it))
                    act.wait_ge(on_v.sem, on_v.at("y3", l))
                    for d in range(2):
                        if d:
                            V("bh0")
                            V("f0")
                            Q("kd0")
                            Q("zt0")
                        PEw(f"W{d}")
                        done(F(LW, PS[2 * d][:, :], ACT.Tanh, bias=col(DR, b + (DRV["w0h"] + 4 * d)), scale=0.5), f"W{d}")
                        PEw(f"A{d}")
                        done(F(AA, PS[2 * d + 1][:, :], ACT.Tanh, bias=col(DR, b + (DRV["a0h"] + 4 * d)), scale=0.5), f"A{d}")
                        if d:
                            PEw("G")
                            done(F(mix(GATE), PS[4][:, :], ACT.Identity), "gate")
                        V(f"cc{d}")
                        if d:
                            Q("kt0")
                            Q("rt0")
                        done(F(PI, CW, ACT.Exp, scale=-1.0), f"Pi{d}")
                        done(F(PP, CW, ACT.Exp), f"Pp{d}")
                        V(f"ce{d}")
                        done(F(LW, LW, ACT.Exp), f"Pe{d}")
                        V(f"em{d}")
                        done(F(EM[d][:, d:d + 3], EM[d][:, d:d + 3], ACT.Exp), f"em{d}")
                        if d == 0:
                            PEw("VT")
                            done(F(VT, PS[5][:, :].rearrange("p (a b) -> p a b", a=NCH), ACT.Identity), "VT")
                        PEw(f"BT{d}")
                        done(F(BT[d], PS[5][:, :].rearrange("p (a b) -> p a b", a=NCH), ACT.Identity), f"BT{d}")
                        PEw(f"KT{d}")
                        done(F(KT[d], PS[6][:, :].rearrange("p (a b) -> p a b", a=NCH), ACT.Identity), f"KT{d}")
                    PEw("Gk31")
                    for j, s in enumerate(LEVELS[1:]):
                        for g in G4:
                            PEw(f"T{s}{g}")
                            if s > 2:
                                PEw(f"Z{LEVELS[j]}{g}")
                            done(F(TT[g], PS[2 * g][:, :].rearrange("p (a b) -> p a b", a=NCH), ACT.Identity), f"T{s}{g}")
                    for s in range(NCH):
                        PEw(f"R{s}")
                        if s:
                            PEw(f"SA{s - 1}")
                        done(F(RHS.rearrange("p d (e v) -> p d e v", e=2), own(0 if s % 2 == 0 else 4), ACT.Identity), f"R{s}")
                    PEw(f"Y{NCH - 1}")
                    done(F(PP, PS[3][:, :], ACT.Identity), "Yev")
                    V("yc")
                    done(F(sq[0], PP, ACT.Square), "gsq")
                    PEw("GV")
                    done(F(sq[1], PS[6][:, :], ACT.Ln, bias=k_gneps, scale=1.0 / 64), "gln")
                    A("gln")
                    done(F(sq[0], sq[1], ACT.Exp, scale=-0.5), "grs")
                norm(2 * l + 1, 24)
                with act.Fori(0, NF // 2) as i:
                    it = l * (NF // 2) + i
                    for q in range(2):
                        act.wait_ge(up_p.sem, up_p.at(f"g{q}", it))
                        act.wait_ge(up_v.sem, up_v.before(f"s{q}", it))
                        F(CV[q], PS[2 * q][:, :], ACT.Identity, bias=col(PR, i * 2 + (PRM["conv_b"] + q)),
                          scale=col(PR, i * 2 + (PRM["conv_w"] + NF + q))).then_inc(up_a.sem, up_a.one(f"cv{q}"))
                    for q in range(2):
                        act.wait_ge(up_v.sem, up_v.at(f"c2{q}", it))
                        act.wait_ge(up_v.sem, up_v.before(f"a{q}", it))
                        F(TH[q], CV[q], ACT.Tanh, scale=0.5).then_inc(up_a.sem, up_a.one(f"th{q}"))
            norm(2 * DEPTH, False)

        @block.vector
        def _(dve):
            credit(dve, [x_ready, ada_done, pro_v, nrm_v, lay_v, in_v, rkv_v, sta_v, att_v, on_v, rw_v, up_v])
            TSC, TTT, STT = dve.tensor_scalar, dve.tensor_tensor, dve.scalar_tensor_tensor
            dve.wait_ge(const_in, 32)
            dve.wait_ge(ada_in[0], 16)
            dve.wait_ge(ada_in[1], 16)
            two_pi = 2 * np.pi
            p1 = 6.28125
            p2 = float(np.round((two_pi - p1) * 2 ** 21) / 2 ** 21)
            p3 = float(two_pi - p1 - p2)
            turn, magic, limit = float(1 / two_pi), 1.5 * 2 ** 23, 3.1415925
            n = [0]

            def pro(ins):
                ins.then_inc(pro_v.sem, pro_v.one(f"s{n[0]}"))
                dve.wait_ge(pro_v.sem, pro_v.at(f"s{n[0]}", 0))
                n[0] += 1

            ang, rnd = RS[:, 0:SEQ], RS[:, SEQ:2 * SEQ]
            pro(dve.tensor_copy(LEV[:, :], LEV_IN.bitcast(I32)))
            pro(dve.tensor_copy(ang, WORK[:, 19456:19968].bitcast(I32)))
            pro(TSC(ang, ang, CST[:, K_FREQ:K_FREQ + 1], None, ALU.mult))
            for dst, quarter in ((sin, 0.0), (cos, 0.25)):
                pro(TSC(rnd, ang, turn, quarter, ALU.mult, ALU.add))
                pro(TSC(rnd, rnd, magic, None, ALU.add))
                pro(TSC(rnd, rnd, magic, None, ALU.subtract))
                pro(STT(dst, rnd, -p1, ang, ALU.mult, ALU.add))
                pro(STT(dst, rnd, -p2, dst, ALU.mult, ALU.add))
                pro(STT(dst, rnd, -p3, dst, ALU.mult, ALU.add))
                if quarter:
                    TSC(dst, dst, float(np.pi / 2), limit, ALU.add, ALU.min).then_inc(pro_v.sem, pro_v.one("s15"))
                    dve.wait_ge(pro_v.sem, pro_v.at("s15", 0))
                    TSC(dst, dst, -limit, None, ALU.max).then_inc(pro_v.sem, pro_v.one("s16"))
                else:
                    TSC(dst, dst, limit, -limit, ALU.min, ALU.max)
                    n_ = n[0]
                    assert n_ == 9
            dve.wait_ge(pro_a.sem, pro_a.at("tanh", 0))
            TSC(sin, sin, CST[:, K_SIGN:K_SIGN + 1], None, ALU.mult)
            STT(CACT, ADA[0], 1.0, CACT, ALU.add, ALU.mult).then_inc(cact_done, 1)
            dve.wait_ge(cact_done, 1)

            def ada_cols(j, use, rnd):
                if not (isinstance(rnd, int) and rnd == 0):
                    dve.wait_ge(mod_kept, rnd)
                for u in range(2):
                    dve.wait_ge(ada_in[u], (use + 2) * 16)
                    dve.tensor_tensor_reduce(out=ADA[u], in0=ADA[u], in1=CACT, scale=0.5, scalar=0.0, op0=ALU.mult,
                                             op1=ALU.add, accum_out=dots[:, u:u + 1]).then_inc(ada_done.sem, ada_done.one(f"a{u}"))
                dve.wait_ge(ada_done.sem, ada_done.at("a1", rnd))
                dve.tensor_copy(MODR[:, bass.ds(j, 2)] if not isinstance(j, int) else MODR[:, j:j + 2], dots[:, :]).then_inc(
                    mod_kept, 1)

            for j in range(8):
                ada_cols(2 * j, j, j)
            dve.wait_ge(x_in, 16)
            dve.sem_inc(x_ready.sem, KD)
            x_ready.turn += KD

            def norm_rows(n, sc):
                dve.wait_ge(nrm_a.sem, nrm_a.at("rstd", n))
                for k in range(KD):
                    STT(hk(k), xk(k), MOD[:, sc + k:sc + k + 1], rs[1], ALU.mult, ALU.mult).then_inc(nrm_v.sem, nrm_v.one(f"h{k}"))

            def shift(bank, dst, j, s, a, b, rnd):
                STT(dst[:, 1:SEQ], PS[bank][:, 0:SEQ - 1], col(PR, j + PRM["mu0"]), dst[:, 1:SEQ], ALU.mult, ALU.add).then_inc(s.sem, s.one(a))
                dve.wait_ge(s.sem, s.at(a, rnd))
                return STT(dst[:, 0:SEQ - 1], PS[bank][:, 1:SEQ], col(PR, j + PRM["mu1"]), dst[:, 0:SEQ - 1], ALU.mult, ALU.add)

            with dve.Fori(0, DEPTH) as l:
                dve.wait_ge(prm_in, (l + 1) * 16)
                dve.wait_ge(mod_kept, l * 24 + 8)

                def lay(ins, name):
                    ins.then_inc(lay_v.sem, lay_v.one(name))
                    dve.wait_ge(lay_v.sem, lay_v.at(name, l))

                pcol = lambda n, w: PR[:, PRM[n]:PRM[n] + w]
                dcol = lambda n, w: DR[:, DRV[n]:DRV[n] + w]
                lay(TTT(MOD[:, 0:16], MODR[:, 0:16], PR[:, 0:16], ALU.add), "modA")
                lay(TSC(MOD[:, 8:16], MOD[:, 8:16], 1.0, None, ALU.add), "modA1")
                lay(TSC(dcol("w0h", 16), pcol("w0", 16), 0.5, None, ALU.mult), "w0h")
                lay(TSC(dcol("ka_h", 4), pcol("k_a", 4), 0.5, None, ALU.mult), "kah")
                lay(TSC(dcol("ka_c", 4), pcol("k_a", 4), -0.5, 1.0, ALU.mult, ALU.add), "kac")
                lay(TSC(dcol("r_kh", 4), pcol("r_k", 4), 0.5, None, ALU.mult), "rkh")
                lay(TTT(dcol("mu_c", 15), pcol("mu0", 15), pcol("mu1", 15), ALU.add), "mu01")
                lay(TSC(dcol("mu_c", 15), dcol("mu_c", 15), -1.0, 1.0, ALU.mult, ALU.add), "muc")
                norm_rows(2 * l, 8)
                for j, name in enumerate(("xw", "xa", "xg")):
                    dve.wait_ge(in_a.sem, in_a.at(name, l))
                    shift(4 + j, mix((XW, XA, XG)[j]), j, in_v, f"{name}1", f"{name}2", l).then_inc(in_v.sem, in_v.one(f"{name}2"))
                    ada_cols(16 + 2 * j, l * 24 + (8 + j), l * 24 + (8 + j))
                dve.wait_ge(in_a.sem, in_a.at("txg", l))
                TSC(mix(XG), mix(XG), 1.0, 0.5, ALU.add, ALU.mult).then_inc(in_v.sem, in_v.one("sxg"))
                with dve.Fori(0, RB) as b:
                    for i, name in enumerate("rkv"):
                        dve.wait_ge(rkv_a.sem, rkv_a.at(name, l * RB + b))
                        shift(4 + i, MIX[:, bass.ds(b * SEQ + 4 * i * SEQ, SEQ)], b * 3 + (3 + i), rkv_v, f"{name}1", f"{name}2",
                              l * RB + b).then_inc(rkv_v.sem, rkv_v.one(f"{name}2"))
                        ada_cols(b * 6 + (22 + 2 * i), l * 24 + b * 3 + (11 + i), l * 24 + b * 3 + (11 + i))
                ada_cols(46, l * 24 + 23, l * 24 + 23)
                dve.wait_ge(mod_kept, l * 24 + 24)
                lay(TTT(MOD[:, 16:48], MODR[:, 16:48], PR[:, 16:48], ALU.add), "modB")
                lay(TSC(MOD[:, 32:40], MOD[:, 32:40], 1.0, None, ALU.add), "modB1")
                dve.wait_ge(rkv_v.sem, rkv_v.at("v2", l * RB + RB - 1))
                for b in range(RB):
                    TSC(mix(KK0 + b), mix(K0 + b), PR[:, PRM["k_k"] + b:PRM["k_k"] + b + 1], None, ALU.mult).then_inc(
                        sta_v.sem, sta_v.one(f"kk{b}"))
                dve.wait_ge(sta_p.sem, sta_p.at("perm", l))
                TTT(KT1, RAW[:, 3, :], cos, ALU.mult).then_inc(sta_v.sem, sta_v.one("kp1"))
                TTT(KT2, PS[6][:, :], sin, ALU.mult).then_inc(sta_v.sem, sta_v.one("kp2"))
                dve.wait_ge(sta_v.sem, sta_v.at("kp2", l))
                TTT(KPE, KT1, KT2, ALU.add).then_inc(sta_v.sem, sta_v.one("kp3"))
                dve.wait_ge(sta_a.sem, sta_a.at("rs0", l))
                for k in range(2):
                    STT(LAT[:, k, :], RAW[:, k, :], PR[:, PRM["q_gain"] + k:PRM["q_gain"] + k + 1], rs[1], ALU.mult, ALU.mult).then_inc(
                        sta_v.sem, sta_v.one(f"qn{k}"))
                dve.wait_ge(sta_a.sem, sta_a.at("rs1", l))
                STT(LAT[:, 2, :], RAW[:, 2, :], PR[:, PRM["kv_gain"]:PRM["kv_gain"] + 1], rs[1], ALU.mult, ALU.mult).then_inc(
                    sta_v.sem, sta_v.one("kvn"))
                for b in range(RB):
                    dve.wait_ge(sta_a.sem, sta_a.at(f"rs{2 + b}", l))
                    TTT(mix(KK0 + b), mix(KK0 + b), rs[1], ALU.mult).then_inc(sta_v.sem, sta_v.one(f"kkn{b}"))
                with dve.Fori(0, HEADS // 2) as hp:
                    it = l * 2 + hp
                    for j, name in enumerate(("kA", "kB")):
                        dve.wait_ge(att_p.sem, att_p.at(name, it))
                        dve.tensor_copy(KN[:, j, :], PS[3 + j][:, :]).then_inc(att_v.sem, att_v.one(name))
                    for j in range(2):
                        dve.wait_ge(att_p.sem, att_p.at(f"v{j}", it))
                        dve.tensor_copy(VT_A[:, 2 * j:2 * j + 2, :], PS[5 + j][:, :].rearrange("p (a b) -> p a b", a=2)).then_inc(
                            att_v.sem, att_v.one(f"v{j}"))
                    dve.wait_ge(att_p.sem, att_p.at("perm", it))
                    dve.wait_ge(att_a.sem, att_a.at("qp", it))
                    TTT(KT1, QPR, cos, ALU.mult).then_inc(att_v.sem, att_v.one("rp1"))
                    TTT(KT2, PS[7][:, :], sin, ALU.mult).then_inc(att_v.sem, att_v.one("rp2"))
                    dve.wait_ge(att_v.sem, att_v.at("rp2", it))
                    TTT(QPE, KT1, KT2, ALU.add).then_inc(att_v.sem, att_v.one("rp3"))
                    for i in range(9):
                        if i < 8:
                            dve.wait_ge(att_p.sem, att_p.at(f"sc{i}", it))
                            dve.tensor_reduce(nmax[:, i:i + 1], PS[i % 2][:, :], AX.X, ALU.max).then_inc(att_v.sem, att_v.one(f"mx{i}"))
                            dve.wait_ge(att_v.sem, att_v.at(f"mx{i}", it))
                            TSC(nmax[:, i:i + 1], nmax[:, i:i + 1], -1.0, None, ALU.mult).then_inc(att_v.sem, att_v.one(f"nm{i}"))
                        if i >= 1:
                            dve.wait_ge(att_a.sem, att_a.at(f"ex{i - 1}", it))
                            dve.reciprocal(rsum[:, i - 1:i], rsum[:, i - 1:i]).then_inc(att_v.sem, att_v.one(f"rc{i - 1}"))
                        if i in (4, 8):
                            e = i // 4 - 1
                            dve.wait_ge(att_p.sem, att_p.at(f"pv{e}", it))
                            dve.tensor_copy(Y[:, bass.ds(hp * (2 * SEQ) + e * SEQ, SEQ)], PS[4 + e][:, :]).then_inc(
                                att_v.sem, att_v.one(f"o{e}"))
                dve.wait_ge(on_a.sem, on_a.at("rs", l))
                for i in range(4):
                    STT(yk(i), yk(i), PR[:, PRM["out_gain"] + i:PRM["out_gain"] + i + 1], rs[1], ALU.mult, ALU.mult).then_inc(
                        on_v.sem, on_v.one(f"y{i}"))
                with dve.Fori(0, RB) as b:
                    it = l * RB + b
                    PEw = lambda n: dve.wait_ge(rw_p.sem, rw_p.at(n, it))
                    A = lambda n: dve.wait_ge(rw_a.sem, rw_a.at(n, it))
                    Q = lambda n: dve.wait_ge(rw_q.sem, rw_q.at(n, it))
                    V = lambda n: dve.wait_ge(rw_v.sem, rw_v.at(n, it))

                    def done(ins, name):
                        ins.then_inc(rw_v.sem, rw_v.one(name))

                    dve.wait_ge(rw_q.sem, rw_q.before("gt", it))
                    kk_b = at(MIX, b + KK0)
                    for d in range(2):
                        A(f"W{d}")
                        done(TSC(LW, LW, 1.0, DECAY / 2, ALU.add, ALU.mult), f"lw{d}")
                        V(f"lw{d}")
                        if d:
                            A("Pp0")
                            V("em0")
                        if d == 0:
                            done(dve.tensor_tensor_scan(CW, scan_mask, LW, 0.0, ALU.mult, ALU.add), "cw0")
                        else:
                            done(dve.tensor_tensor_scan(CW[:, ::-1], scan_mask, LW[:, ::-1], 0.0, ALU.mult, ALU.add), "cw1")
                        V(f"cw{d}")
                        cw4 = CW.rearrange("p (c t) -> p c t", c=NCH)
                        mid, end = (63, 127) if d == 0 else (64, 0)
                        done(dve.tensor_copy(MID[d], cw4[:, :, mid]), f"mid{d}")
                        V(f"mid{d}")
                        done(TTT(cw4, cw4, MID[d].unsqueeze(2).to_broadcast([P, NCH, C]), ALU.subtract), f"cc{d}")
                        V(f"cc{d}")
                        done(TTT(LW, CW, LW, ALU.subtract), f"ce{d}")
                        if d == 0:
                            done(TTT(EM[0][:, 0:3], cw4[:, 0:3, end], MID[0][:, 1:4], ALU.add), "em0")
                        else:
                            done(TTT(EM[1][:, 1:4], cw4[:, 1:4, end], MID[1][:, 0:3], ALU.add), "em1")
                        A(f"A{d}")
                        done(STT(BB, AA, 1.0, kk_b, ALU.add, ALU.mult), f"b1{d}")
                        V(f"b1{d}")
                        A(f"Pi{d}")
                        done(STT(BH[d], BB, -0.5, PI, ALU.mult, ALU.mult), f"bh{d}")
                        done(TSC(AA, AA, col(DR, b + DRV["ka_h"]), col(DR, b + DRV["ka_c"]), ALU.mult, ALU.add), f"f{d}")
                        for g in (2 * d, 2 * d + 1):
                            for m, dst in enumerate((GB[g], GK[g])):
                                for h in range(2):
                                    name = f"{('Gb', 'Gk')[m]}{g}{h}"
                                    PEw(name)
                                    done(TTT(dst[:, 2 * h:2 * h + 2, :, :].rearrange("p a b c -> p a (b c)"),
                                             PS[2 * m + h][:, :].rearrange("p (a b) -> p a b", a=2),
                                             gmask[d].unsqueeze(1).to_broadcast([P, 2, 256]), ALU.mult), name)
                    Q("kbs")
                    done(STT(LW, KDD[0], col(DR, b + DRV["r_kh"]), at(MIX, b + R0), ALU.mult, ALU.mult), "kbr")
                    PEw("BON")
                    done(TTT(mix(BON), PS[7][:, :], VB, ALU.mult), "bon")
                    for g in G4:
                        PEw(f"LT{g}")
                        Q(f"ZI{g}")
                        settle(dve, "dve")
                        done(dve.copy_predicated(XX[g], level_mask(1, g // 2, False), PS[2 * g + 1][:, :].rearrange("p (a b) -> p a b", a=NCH)), f"X1{g}")
                        done(dve.copy_predicated(XT[g], level_mask(1, g // 2, True), GB[g][:, :, 0, :]), f"Z1{g}")
                    for s in LEVELS[1:]:
                        for g in G4:
                            if s < 64:
                                PEw(f"X{s}{g}")
                                settle(dve, "dve")
                                done(dve.copy_predicated(XX[g], level_mask(s, g // 2, False), PS[2 * g + 1][:, :].rearrange("p (a b) -> p a b", a=NCH)), f"X{s}{g}")
                            PEw(f"Z{s}{g}")
                            settle(dve, "dve")
                            done(dve.copy_predicated(XT[g], level_mask(s, g // 2, True), PS[2 * g][:, :].rearrange("p (a b) -> p a b", a=NCH)), f"Z{s}{g}")
                    for s in range(NCH):
                        ch = (s, NCH - 1 - s)
                        if 0 < s < NCH - 1:
                            for d in range(2):
                                last = TSC(SMD[:, d, :], SM[:, d, :], EM[d][:, ch[d]:ch[d] + 1], None, ALU.mult)
                            done(last, f"SD{s}")
                        PEw(f"SA{s}")
                        if s:
                            PEw(f"Y{s - 1}")
                        done(dve.tensor_copy(SA.rearrange("p d (e v) -> p d e v", e=2), own(1)), f"SA{s}")
                        if s < NCH - 1:
                            PEw(f"S{s}")
                            for d in range(2):
                                if s == 0:
                                    A(f"em{d}")
                                done(STT(SM[:, d, :], PS[2][:, d * P:(d + 1) * P], EM[d][:, ch[d]:ch[d] + 1], head_ones, ALU.mult,
                                         ALU.mult), f"S{s}{d}")
                            V(f"S{s}1")
                            if s:
                                done(TTT(SM, SM, SMD, ALU.add), f"SS{s}")
                                V(f"SS{s}")
                    PEw("GM")
                    done(STT(PP, PS[5][:, :], -1.0 / 64, PP, ALU.mult, ALU.add), "yc")
                    A("grs")
                    done(STT(PP, PP, col(PR, b + PRM["gn_g"]), sq[0], ALU.mult, ALU.mult), "gn1")
                    V("gn1")
                    done(STT(PP, PP, col(PR, b + PRM["gn_b"]), mix(BON), ALU.add, ALU.add), "gn2")
                for m in range(KD):
                    dve.wait_ge(tile_done.sem, l * NTILE + (NPROJ + m + 1 + 3))
                    STT(xk(m), PS[m % 4][:, :], MOD[:, 16 + m:17 + m], xk(m), ALU.mult, ALU.add).then_inc(x_ready.sem, x_ready.one(f"x{m}"))
                norm_rows(2 * l + 1, 32)
                with dve.Fori(0, NF // 2) as i:
                    it = l * (NF // 2) + i
                    for q in range(2):
                        dve.wait_ge(up_a.sem, up_a.at(f"cv{q}", it))
                        STT(CV[q][:, 1:SEQ], PS[2 * q][:, 0:SEQ - 1], col(PR, i * 2 + (PRM["conv_w"] + q)), CV[q][:, 1:SEQ], ALU.mult,
                            ALU.add).then_inc(up_v.sem, up_v.one(f"c1{q}"))
                        dve.wait_ge(up_v.sem, up_v.at(f"c1{q}", it))
                        STT(CV[q][:, 0:SEQ - 1], PS[2 * q][:, 1:SEQ], col(PR, i * 2 + (PRM["conv_w"] + 2 * NF + q)), CV[q][:, 0:SEQ - 1],
                            ALU.mult, ALU.add).then_inc(up_v.sem, up_v.one(f"c2{q}"))
                    for q in range(2):
                        dve.wait_ge(up_a.sem, up_a.at(f"th{q}", it))
                        STT(TH[q], TH[q], 1.0, CV[q], ALU.add, ALU.mult).then_inc(up_v.sem, up_v.one(f"s{q}"))
                        dve.wait_ge(up_v.sem, up_v.at(f"s{q}", it))
                        dve.wait_ge(up_p.sem, up_p.at(f"v{q}", it))
                        STT(MIX[:, bass.ds(i * (2 * SEQ) + q * SEQ, SEQ)], PS[2 * q + 1][:, :], 0.5, TH[q], ALU.mult,
                            ALU.mult).then_inc(up_v.sem, up_v.one(f"a{q}"))
                with dve.Fori(0, KD // 2) as i:
                    it = l * (KD // 2) + i
                    for q in range(2):
                        ada_cols(i * 4 + 2 * q, l * 24 + i * 2 + (24 + q), l * 24 + i * 2 + (24 + q))
                        dve.wait_ge(down_p.sem, down_p.at(f"m{q}", it))
                        xm = X[:, bass.ds(i * (2 * SEQ) + q * SEQ, SEQ)]
                        STT(xm, PS[4 + q][:, :], col(MOD, i * 2 + (40 + q)), xm, ALU.mult, ALU.add).then_inc(
                            x_ready.sem, x_ready.one(f"x{x_ready.turn % KD}"))
                x_ready.turn = 0
            dve.wait_ge(nrm_a.sem, nrm_a.at("rstd", 2 * DEPTH))
            for k in range(KD):
                STT(xk(k), xk(k), CST[:, K_GAIN + k:K_GAIN + k + 1], rs[1], ALU.mult, ALU.mult).then_inc(
                    x_ready.sem, x_ready.one(f"x{k}"))

        @block.gpsimd
        def _(pool):
            credit(pool, [att_q, rw_q])
            pool.dma_start(WORK[:, 19456:19968].bitcast(I32), pos.partition_broadcast(P)).then_inc(ada_in[0], 16)
            pool.dma_start(CACT, c.partition_broadcast(P)).then_inc(ada_in[1], 16)

            def load_ada(layer, j, slot, seq):
                pool.wait_ge(ada_done.sem, seq + 1)
                settle(pool, "pool")
                pool.dma_start(ADA[slot], ada[layer, j]).then_inc(ada_in[slot], 16)

            pool.wait_ge(cact_done, 1)
            for j in range(16):
                load_ada(0, j, j % 2, j)

            with pool.Fori(0, DEPTH) as l:
                with pool.Fori(0, 16) as i:
                    for u in range(2):
                        load_ada(l, i * 2 + (16 + u), u, l * 48 + i * 2 + (16 + u))
                with pool.Fori(0, HEADS // 2) as hp:
                    it = l * 2 + hp
                    for i in range(8):
                        pool.wait_ge(att_v.sem, att_v.at(f"rc{i}", it))
                        settle(pool, "pool")
                        pool.tensor_scalar(PB[:, i % 2, :], PB[:, i % 2, :], rsum[:, i:i + 1], None, ALU.mult).then_inc(
                            att_q.sem, att_q.one(f"pn{i}"))
                pool.wait_ge(att_p.sem, att_p.at("pv1", l * 2 + 1))
                settle(pool, "pool")
                with pool.Fori(0, RB) as b:
                    it = l * RB + b
                    PEw = lambda n: (pool.wait_ge(rw_p.sem, rw_p.at(n, it)), settle(pool, "pool"))
                    A = lambda n: (pool.wait_ge(rw_a.sem, rw_a.at(n, it)), settle(pool, "pool"))
                    V = lambda n: (pool.wait_ge(rw_v.sem, rw_v.at(n, it)), settle(pool, "pool"))
                    Q = lambda n: (pool.wait_ge(rw_q.sem, rw_q.at(n, it)), settle(pool, "pool"))
                    TTT = pool.tensor_tensor

                    def done(ins, name):
                        ins.then_inc(rw_q.sem, rw_q.one(name))

                    pool.wait_ge(rw_p.sem, rw_p.before("GV", it))
                    pool.wait_ge(rw_v.sem, rw_v.before("gn2", it))
                    settle(pool, "pool")
                    done(pool.tensor_copy(VB, at(MIX, b + V0)), "vb")
                    for d in range(2):
                        half = lambda z: ZR[d][:, :, z, :]
                        v4 = lambda ap: ap.rearrange("p (c t) -> p c t", c=NCH)
                        A(f"Pp{d}")
                        done(TTT(half(1), v4(at(MIX, b + R0)), v4(PP), ALU.mult), f"rt{d}")
                        A(f"Pe{d}")
                        done(TTT(half(0), v4(at(MIX, b + KK0)), v4(LW), ALU.mult), f"zt{d}")
                        V(f"f{d}")
                        done(TTT(KDD[d], at(MIX, b + K0), AA, ALU.mult), f"kd{d}")
                        Q(f"kd{d}")
                        done(TTT(KH[d], KDD[d], PI, ALU.mult), f"kt{d}")
                    done(TTT(KDD[0], KDD[0], KDD[1], ALU.add), "kbs")
                    PEw("BON")
                    for g in G4:
                        if g == 0:
                            V("f1")
                            A("em1")
                            Q("kbs")
                        done(pool.tensor_copy(XX[g], ident.unsqueeze(1).to_broadcast([P, NCH, P])), f"XI{g}")
                        done(pool.tensor_copy(XT[g], ident.unsqueeze(1).to_broadcast([P, NCH, P])), f"ZI{g}")
                    V("gn2")
                    done(TTT(at(Y, b + 4), PP, mix(GATE), ALU.mult), "gt")
                pool.wait_ge(rw_v.sem, rw_v.at("gn2", l * RB + RB - 1))
                pool.wait_ge(rw_q.sem, rw_q.at("gt", l * RB + RB - 1))
                settle(pool, "pool")
                with pool.Fori(0, 8) as i:
                    for u in range(2):
                        load_ada(1 - l, i * 2 + u, u, l * 48 + i * 2 + (48 + u))
            for u in range(2):
                pool.wait_ge(ada_in[u], 16 * (1 + 8 + 24 * DEPTH))


def _blocks(w, starts, width=P):
    rows = w.shape[0]
    return np.stack([w[:, s:s + width].reshape(rows // P, P, width).transpose(1, 0, 2) for s in starts])


def _columns(v):
    return np.ascontiguousarray(v.reshape(-1, P).T)


def _constants():
    cst = np.zeros((P, NCST), np.float32)
    i = np.arange(P)
    cst[:, K_ID:K_ID + P] = np.eye(P)
    cst[:, K_ONE:K_ONE + P] = 1
    cst[:, K_BD:K_BD + P] = i[:, None] // 64 == i[None, :] // 64
    cst[i, K_SWAP + (i ^ 32)] = 1
    for d, (strict, incl) in enumerate(((i[None] > i[:, None], i[None] >= i[:, None]),
                                        (i[None] < i[:, None], i[None] <= i[:, None]))):
        cst[:, K_GF + 256 * d:K_GF + 256 * d + P] = strict
        cst[:, K_GF + 256 * d + P:K_GF + 256 * d + 256] = incl
    cst[:, K_SCAN:K_SCAN + SEQ] = np.arange(SEQ) % C != 0
    half = ROPE // 2
    cst[:, K_FREQ] = (np.float32(10000.0) ** (-np.arange(half, dtype=np.float32) / np.float32(half)))[i % half]
    cst[:, K_SIGN] = np.where(i % 64 < 32, -1, 1)
    cst[:, K_EPS], cst[:, K_GNEPS], cst[:, K_KKEPS] = EPS, GN_EPS, KK_EPS
    lev = np.zeros((P, len(LEVELS), 2, P), np.int32)
    for j, s in enumerate(LEVELS):
        low = ((i[:, None] // (2 * s) == i[None] // (2 * s)) & (i[:, None] % (2 * s) >= s) & (i[None] % (2 * s) < s))
        lev[:, j, 0], lev[:, j, 1] = low, low.T
    return cst, lev.reshape(P, -1)


def kernel(**inputs):
    import concourse.bacc as bacc
    from concourse.bass_utils import run_bass_kernel_spmd

    a = {k: np.asarray(v) for k, v in inputs.items()}
    cst, lev = _constants()
    cst[:, K_GAIN:K_GAIN + KD] = _columns(a["final_norm"])
    arrays = {"x_dram": np.ascontiguousarray(a["x"][0].T.reshape(KD, P, SEQ).transpose(1, 0, 2)),
              "c_dram": a["c"].reshape(1, DM), "pos_dram": a["positions"].reshape(1, SEQ),
              "cst_dram": cst, "lev_dram": lev}
    prm, tiles, up, down, ada, mlaw, lora = [], [], [], [], [], [], []
    base = 448
    for l in range(DEPTH):
        win = a["w_in"][l]
        kpe = np.concatenate([win[:, :384], win[:, 384:448], win[:, 384:448], win[:, base + 1536:]], axis=1)
        rkv = win[:, base:base + 1536]
        tiles.append(np.concatenate([_blocks(kpe, range(0, 896, P)),
                                     _blocks(rkv, [i * 512 + b * P for b in range(RB) for i in range(3)]),
                                     _blocks(a["w_out"][l], range(0, DM, P))]))
        wu = a["ffn_w_up"][l]
        g, v = _blocks(wu[:, :FF], range(0, FF, P)), _blocks(wu[:, FF:], range(0, FF, P))
        up.append(np.stack([g, v], axis=3))
        down.append(_blocks(a["ffn_w_down"][l], range(0, DM, P)))
        ada.append(a["ada_w"][l].T.reshape(48, P, DM))
        uq = a["mla_w_uq"][l].reshape(2, P, HEADS, NOPE + ROPE)
        ukv = a["mla_w_ukv"][l].reshape(P, HEADS, NOPE + VD)
        pairs = []
        for hp in range(2):
            h0, h1 = 2 * hp, 2 * hp + 1
            q = np.concatenate([uq[:, :, h0, :NOPE], uq[:, :, h1, :NOPE], uq[:, :, h0, NOPE:], uq[:, :, h1, NOPE:]], axis=2)
            kv = np.concatenate([ukv[:, h0, :NOPE], ukv[:, h1, :NOPE], ukv[:, h0, NOPE:], ukv[:, h1, NOPE:]], axis=1)
            pairs.append(np.concatenate([q[0], q[1], kv], axis=1))
        mlaw.append(np.stack(pairs))
        w2, a2, g2 = a["rwkv_w2"][l].reshape(P, RW), a["rwkv_a2"][l].reshape(P, RW), a["rwkv_g2"][l]
        lora.append(np.stack([np.stack([m[:, b * P:(b + 1) * P] for m in (w2, a2, g2)], axis=1) for b in range(RB)]))
        mu = a["rwkv_mu"][l]
        order = [1536, 1664, 1792] + [i * 512 + b * P for b in range(RB) for i in range(3)]
        mus = [np.stack([mu[j][s:s + P] for s in order], axis=1) for j in range(2)]
        prm.append(np.concatenate(
            [_columns(a["ada_b"][l]), _columns(a["mla_q_norm"][l]), _columns(a["mla_kv_norm"][l]),
             _columns(a["mla_out_norm"][l]), mus[0], mus[1], _columns(a["rwkv_w0"][l].reshape(-1)),
             _columns(a["rwkv_a0"][l].reshape(-1)), _columns(a["rwkv_k_k"][l]), _columns(a["rwkv_k_a"][l]),
             _columns(a["rwkv_r_k"][l].reshape(-1)), _columns(a["rwkv_gn_g"][l]), _columns(a["rwkv_gn_b"][l]),
             _columns(a["ffn_conv_w"][l].reshape(-1)), _columns(a["ffn_conv_b"][l])], axis=1))
    tiles.append(tiles[0][:3])
    arrays |= {"prm_dram": np.stack(prm), "tiles_dram": np.concatenate(tiles), "up_dram": np.concatenate(up),
               "down_dram": np.concatenate(down), "ada_dram": np.stack(ada), "mlaw_dram": np.stack(mlaw),
               "lora_dram": np.stack(lora)}
    arrays = {k: np.ascontiguousarray(v) for k, v in arrays.items()}

    nc = bacc.Bacc("TRN2", target_bir_lowering=False, num_devices=1)
    aps = {n: nc.dram_tensor(n, v.shape, mybir.dt.from_np(v.dtype), kind="ExternalInput").ap() for n, v in arrays.items()}
    out = nc.dram_tensor("out_dram", (KD, P, SEQ), F32, kind="ExternalOutput").ap()
    names = ("x", "c", "pos", "cst", "lev", "prm", "tiles", "up", "down", "ada", "mlaw", "lora")
    trunk(nc, *[aps[f"{n}_dram"] for n in names], out)
    r = run_bass_kernel_spmd(nc, [arrays], core_ids=[0])
    got = np.asarray(r.results[0]["out_dram"])
    return np.ascontiguousarray(got.transpose(2, 0, 1).reshape(1, SEQ, DM))
```

```python
import numpy as np

import concourse.bass as bass
from concourse import mybir
from contextlib import ExitStack

F32 = mybir.dt.float32
F32R = mybir.dt.float32r
I32 = mybir.dt.int32
U8 = mybir.dt.uint8
ALU = mybir.AluOpType
ACT = mybir.ActivationFunctionType
AX = mybir.AxisListType

P = 128
DM, SEQ, DEPTH = 1024, 512, 2
KD = DM // P
HEADS, NOPE, ROPE, VD = 4, 128, 64, 128
QR, KVR = 256, 128
QB = KVR_B = 2
RW = 512
RB = RW // P
C = 128
NCH = SEQ // C
FF = 2816
NF = FF // P
EPS, GN_EPS, KK_EPS = 1e-6, 64e-5, 1e-12
DECAY = -float(np.exp(-0.5))
SCALE = (NOPE + ROPE) ** -0.5
NPROJ = 19
NTILE = NPROJ + KD
NUP, NDN = NF, NF // 2
NMLP = NUP + NDN
DN_BANK = [7, 4, 5, 6, 0, 1, 2, 3]
LEVELS = [1, 2, 4, 8, 16, 32, 64]

_SIZES = [("ada_b", 48), ("q_gain", 2), ("kv_gain", 1), ("out_gain", 4), ("mu0", 15), ("mu1", 15),
          ("w0", 8), ("a0", 8), ("k_k", 4), ("k_a", 4), ("r_k", 4), ("gn_g", 4), ("gn_b", 4),
          ("conv_w", 66), ("conv_b", NF)]
PRM, _n = {}, 0
for _name, _w in _SIZES:
    PRM[_name] = _n
    _n += _w
NPRM = _n
DRV = {"w0h": 0, "a0h": 8, "ka_h": 16, "ka_c": 20, "r_kh": 24, "mu_c": 28}
NDRV = 43
K_ID, K_ONE, K_BD, K_SWAP, K_GF, K_SCAN, K_FREQ, K_SIGN, K_EPS, K_GNEPS, K_KKEPS, K_HEAD, K_NHEAD, K_GAIN = (
    0, 128, 256, 384, 512, 1024, 1536, 1537, 1538, 1539, 1540, 1541, 1543, 1545)
NCST = 1545 + KD


class Steps:

    def __init__(self, sem, names):
        self.sem, self.names, self.turn = sem, names, 0
        self.index = {n: i for i, n in enumerate(names)}
        assert len(self.index) == len(names)

    def one(self, name):
        assert self.names[self.turn % len(self.names)] == name, (name, self.names[self.turn % len(self.names)])
        self.turn += 1
        return 1

    def at(self, name, rnd):
        return (rnd + 1) * len(self.names) + (self.index[name] + 1)

    def before(self, name, rnd):
        return rnd * len(self.names) + (self.index[name] + 1)


def trunk(nc, x, c, pos, cst, lev, prm, tiles, mlp, ada, mlaw, lora, out):
    ctx = ExitStack()
    with ctx:
        def sb(name, cols, dt=F32):
            return ctx.enter_context(nc.sbuf_tensor(name, [P, cols], dt))

        def two_names(name, cols):
            with nc.sbuf_tensor(name, [P, cols], F32) as whole:
                pass
            return whole, sb(name + "_parts", cols, F32R)

        def steps(name, names):
            return Steps(ctx.enter_context(nc.semaphore(name)), names)

        def sem(name):
            return ctx.enter_context(nc.semaphore(name))

        def view(t, off, *dims):
            n = int(np.prod(dims))
            ap = t[:, off:off + n]
            if len(dims) == 2:
                ap = ap.rearrange("p (a b) -> p a b", a=dims[0])
            if len(dims) == 3:
                ap = ap.rearrange("p (a b c) -> p a b c", a=dims[0], b=dims[1])
            if len(dims) == 4:
                ap = ap.rearrange("p (a b c d) -> p a b c d", a=dims[0], b=dims[1], c=dims[2])
            return ap

        X = sb("x_res", KD * SEQ)
        Y, Y_R = two_names("y_mix", KD * SEQ)
        CST = sb("constants", NCST)
        LEV = sb("level_masks", len(LEVELS) * 2 * P, U8)
        PR = sb("params", NPRM)
        DR = sb("derived", NDRV)
        TRIG = sb("cos_sin", 2 * SEQ)
        RING, RING_R = two_names("proj_weights", 3 * KD * P)
        RING_H = sb("proj_weights_hi", 3 * KD * P, F32R)
        SQ = sb("squares", 2 * SEQ)
        RS = sb("rstd", 2 * SEQ)
        MODR = sb("mod_raw", 48)
        MOD = sb("mod", 48)
        MIX, MIX_R = two_names("mixer_inputs", NF * SEQ)
        WORK, WORK_R = two_names("work", 21504)

        PS = [ctx.enter_context(nc.psum_tensor(f"bank{i}", [P, 512], F32)) for i in range(8)]

        xk = lambda k: X[:, k * SEQ:(k + 1) * SEQ]
        yk = lambda k: Y[:, k * SEQ:(k + 1) * SEQ]
        at = lambda t, b: t[:, bass.ds(b * SEQ, SEQ)]
        col = lambda t, i: t[:, bass.ds(i, 1)] if not isinstance(i, int) else t[:, i:i + 1]
        ident = CST[:, K_ID:K_ID + P]
        ones = CST[:, K_ONE:K_ONE + P]
        head_ones = CST[:, K_BD:K_BD + P]
        swap = CST[:, K_SWAP:K_SWAP + P]
        gmask = [CST[:, K_GF + 256 * d:K_GF + 256 * d + 256] for d in range(2)]
        scan_mask = CST[:, K_SCAN:K_SCAN + SEQ]
        k_eps, k_gneps, k_kkeps = CST[:, K_EPS:K_EPS + 1], CST[:, K_GNEPS:K_GNEPS + 1], CST[:, K_KKEPS:K_KKEPS + 1]

        def level_mask(s, d, transposed):
            j = 2 * LEVELS.index(s) + (d ^ int(transposed))
            return LEV[:, j * P:(j + 1) * P].unsqueeze(1).to_broadcast([P, NCH, P])

        cos, sin = TRIG[:, 0:SEQ], TRIG[:, SEQ:2 * SEQ]
        ring = [view(RING, s * KD * P, KD, P) for s in range(3)]
        ring_h = [view(RING_H, s * KD * P, KD, P) for s in range(3)]
        ring_l = [view(RING_R, s * KD * P, KD, P) for s in range(3)]
        plain = lambda ap: ap.bitcast(F32)
        ylk = lambda k: Y_R[:, k * SEQ:(k + 1) * SEQ]
        sq = [SQ[:, i * SEQ:(i + 1) * SEQ] for i in range(2)]
        rs = [RS[:, i * SEQ:(i + 1) * SEQ] for i in range(2)]
        R0, K0, V0, KK0, XW, XA, XG, BON, GATE = 0, 4, 8, 12, 16, 17, 18, 19, 20
        mix = lambda i: MIX[:, i * SEQ:(i + 1) * SEQ]
        H = WORK[:, 0:KD * SEQ]
        hk = lambda k: H[:, k * SEQ:(k + 1) * SEQ]
        hlk = lambda k: WORK_R[:, k * SEQ:(k + 1) * SEQ]
        HH = WORK_R[:, 9472:9472 + KD * SEQ]
        hhk = lambda k: HH[:, k * SEQ:(k + 1) * SEQ]
        MW_IN = [view(WORK, 4096 + i * 2048, 2, KD, P) for i in range(2)]
        MW_L = [view(WORK_R, 4096 + i * 2048, 2, KD, P) for i in range(2)]
        MW_H = [view(Y_R, i * 2048, 2, KD, P) for i in range(2)]
        CV = [WORK[:, 13568 + i * SEQ:13568 + (i + 1) * SEQ] for i in range(2)]
        TH = [WORK[:, 14592 + i * SEQ:14592 + (i + 1) * SEQ] for i in range(2)]
        ADA = [WORK[:, 15872 + i * DM:15872 + (i + 1) * DM] for i in range(2)]
        ACT_H = [view(WORK_R, 17920 + i * 2 * SEQ, 2, SEQ) for i in range(2)]
        ADA0 = [WORK[:, 2048 + i * DM:2048 + (i + 1) * DM] for i in range(8)] + [MIX[:, i * DM:(i + 1) * DM] for i in range(8)]
        POS_IN = WORK[:, 13568:14080]
        TANH_C = WORK[:, 14592:15616]
        LEV_IN = WORK[:, 0:len(LEVELS) * 2 * P]
        CACT = WORK[:, 20480:21504]
        RAW = view(WORK, 4096, 4, SEQ)
        LAT = view(WORK, 6144, 3, SEQ)
        MW = WORK[:, 7680:8960]
        KPE = [WORK[:, 8960:9472], WORK[:, 13568:14080]]
        o = 9472
        QN = view(WORK, o, 2, SEQ)
        QPR = WORK[:, o + 1024:o + 1536]
        QPE = WORK[:, o + 1536:o + 2048]
        KN = view(WORK, o + 2048, 2, SEQ)
        VT_A = view(WORK, o + 3072, 4, 2 * P)
        PB = [WORK[:, 0:512], WORK[:, 512:1024], WORK[:, 14080:14592]]
        LOGS = [WORK[:, o + SEQ * i:o + SEQ * i + SEQ] for i in range(6)]
        PTb = [view(WORK, 17920 - 2048 * (1 - e) , 4, SEQ) for e in range(2)]
        KT1 = WORK[:, 0:512]
        KT2 = WORK[:, 512:1024]
        ZR = [view(WORK, 1024 * d, NCH, 2, C) for d in range(2)]
        BH = [[WORK[:, o + 512 * e:o + 512 * e + 512] for e in range(2)] for o in (2048, 18432)]
        KH = [[WORK[:, 3072 + 512 * e:3584 + 512 * e] for e in range(2)], sq]
        TT = [view(WORK, 2048 + 512 * g, NCH, C) for g in range(4)]
        BT = [view(WORK, 4096 + 512 * d, NCH, P) for d in range(2)]
        KT = [view(WORK, 5120 + 512 * d, NCH, P) for d in range(2)]
        KDD = [WORK[:, 6144 + 512 * d:6656 + 512 * d] for d in range(2)]
        GB = [view(WORK, 7168 + 1024 * g, NCH, 2, C) for g in range(4)]
        GK = [view(WORK, 11264 + 1024 * g, NCH, 2, C) for g in range(4)]
        XX = [view(WORK, 15360 + 512 * g, NCH, C) for g in range(4)]
        XT = [view(WORK, 17408 + 512 * g, NCH, C) for g in range(4)]
        TMP = [WORK[:, 15360 + 512 * i:15872 + 512 * i] for i in range(6)]
        LW, AA, CW, PP, PI, BB = TMP
        VB = WORK[:, 19456:19968]
        VT = view(WORK, 19968, NCH, P)
        RHS = view(RS, 0, 2, P)
        SA = view(RS, 256, 2, P)
        SM = view(RS, 512, 2, P)
        SMD = view(RS, 768, 2, P)
        edges = sb("chunk_edges", 16)
        MID = [edges[:, 4 * d:4 * d + 4] for d in range(2)]
        EM = [edges[:, 8 + 4 * d:12 + 4 * d] for d in range(2)]

        def own(bank, d=None):
            ap = PS[bank][:, :].rearrange("p (d a v) -> p d a v", d=2, a=4)[:, :, 0::3, :]
            return ap if d is None else ap[:, d]
        l_dir = view(MIX, 21 * SEQ, 4, P)
        l_gate = sb("gate_weights", P)
        head = [CST[:, K_HEAD + e:K_HEAD + e + 1] for e in range(2)]
        nhead = [CST[:, K_NHEAD + e:K_NHEAD + e + 1] for e in range(2)]
        dots = sb("ada_dots", 2)
        nmax = sb("neg_max", 8)
        rsum = sb("row_sum", 8)

        x_in, const_in, prm_in = sem("x_in"), sem("const_in"), sem("prm_in")
        ring_in = [sem(f"ring_in{i}") for i in range(3)]
        mlp_in = [sem(f"mlp_in{i}") for i in range(2)]
        ada_in = [sem(f"ada_in{i}") for i in range(2)]
        ada0_in = [sem(f"ada0_in{i}") for i in range(4)]
        pos_in, c_in = sem("pos_in"), sem("c_in")
        mla_in, lora_in, out_done = sem("mla_in"), sem("lora_in"), sem("out_done")
        cact_done, mod_kept = sem("cact_done"), sem("mod_kept")

        x_ready = steps("x_ready", [f"x{k}" for k in range(KD)])
        tile_done = steps("tile_done", [f"t{k}" for k in range(3)])
        ada_done = steps("ada_done", ["a0", "a1"])
        pro_v = steps("pro_v", [f"s{i}" for i in range(17)])
        pro_a = steps("pro_a", ["sin", "cos", "tanh"])
        nrm_a = steps("nrm_a", [f"sq{k}" for k in range(KD)] + ["ln", "rstd"] + [f"h{k}" for k in range(KD)])
        nrm_p = steps("nrm_p", [f"sum{k}" for k in range(KD)])
        nrm_v = steps("nrm_v", ["t0"] + [n for k in range(1, KD) for n in (f"t{k}", f"l{k - 1}")] + [f"l{KD - 1}"])
        spl_a = steps("spl_a", [f"t{k}" for k in range(3)])
        spl_q = steps("spl_q", [f"t{k}" for k in range(3)])
        y_a = steps("y_a", [f"y{k}" for k in range(KD)])
        y_v = steps("y_v", [f"y{k}" for k in range(KD)])
        msp_a = steps("msp_a", ["h0", "h1"])
        msp_q = steps("msp_q", ["l0"])
        msp_v = steps("msp_v", ["l1"])
        act_a = steps("act_a", ["h0", "h1"])
        act_v = steps("act_v", ["l0", "l1"])
        lay_v = steps("lay_v", ["modA", "modA1", "w0h", "kah", "kac", "rkh", "mu01", "muc", "modB", "modB1"])
        in_a = steps("in_a", ["raw0", "raw1", "raw2", "raw3", "xw", "xa", "txw", "xg", "txg"])
        in_v = steps("in_v", ["xw1", "xw2", "xa1", "xa2", "xg1", "xg2", "sxg"])
        rkv_a = steps("rkv_a", ["r", "k", "v"])
        rkv_v = steps("rkv_v", ["r1", "r2", "k1", "k2", "v1", "v2"])
        sta_p = steps("sta_p", [f"s{i}" for i in range(7)] + ["perm"])
        sta_a = steps("sta_a", [f"sq{i}" for i in range(7)] + [f"{w}{i}" for w in ("ln", "rs") for i in range(6)])
        sta_v = steps("sta_v", [f"kk{b}" for b in range(4)] + ["kp1", "kp2", "kp3", "kpm0", "kpm1", "qn0", "qn1", "kvn"]
                      + [f"kkn{b}" for b in range(4)])
        att_a = ["qA", "qB", "qp"]
        att_v = ["kA", "kB", "v0", "v1", "rp1", "rp2", "rp3"]
        att_p = ["qA", "qB", "qp", "kA", "kB", "v0", "v1", "perm"]
        for i in range(10):
            if i < 8:
                att_p.append(f"sc{i}")
                att_v += [f"mx{i}", f"nm{i}"]
                att_a.append(f"ex{i}")
            if 1 <= i < 9:
                att_v += [f"rc{i - 1}", f"pn{i - 1}"]
            if i >= 2:
                att_p.append(f"tr{i - 2}")
                att_a.append(f"pt{i - 2}")
            if i in (6, 9):
                att_p.append(f"pv{i // 9}")
            if i in (7, 9):
                att_v.append(f"o{i // 9}")
        att_a, att_v, att_p = steps("att_a", att_a), steps("att_v", att_v), steps("att_p", att_p)
        on_a = steps("on_a", [f"sq{i}" for i in range(4)] + ["ln", "rs"])
        on_p = steps("on_p", [f"s{i}" for i in range(4)])
        on_v = steps("on_v", [f"y{i}" for i in range(4)])
        G4 = range(4)
        rw_p = ["W0", "A0", "W1", "A1", "G", "VT"]
        for d in range(2):
            rw_p += [f"BT{d}0", f"BT{d}1", f"KT{d}0", f"KT{d}1"]
            for g in (2 * d, 2 * d + 1):
                rw_p += [f"{m}{g}{h}" for m in ("Gb", "Gk") for h in range(2)]
        rw_p += ["BON"] + [f"LT{g}" for g in G4]
        for s in LEVELS[1:]:
            rw_p += [f"T{s}{g}" for g in G4]
            for g in G4:
                rw_p += ([f"X{s}{g}"] if s < 64 else []) + [f"Z{s}{g}"]
        rw_a = ["W0", "A0", "Pi0", "Pp0", "Pe0", "em0", "gate", "VT", "BT00", "BT01",
                "W1", "A1", "KT00", "KT01", "Pi1", "Pp1", "Pe1", "em1", "BT10", "BT11", "KT10", "KT11"]
        rw_a += [f"XI{g}" for g in G4]
        for s in LEVELS[1:]:
            rw_a += [f"T{s}{g}" for g in G4]
        rw_v = []
        for d in range(2):
            rw_v += [f"{n}{d}" for n in ("lw", "cw", "mid", "cc", "ce", "em", "b1", "bh0", "bh1", "f", "kd", "kh0", "kh1")]
        rw_v += [f"{m}{g}{h}" for g in G4 for m in ("Gb", "Gk") for h in range(2)]
        rw_v += ["kbr", "bon"] + [f"ZI{g}" for g in G4] + [f"{m}{g}" for g in G4 for m in ("X1", "Z1")]
        for s in LEVELS[1:]:
            for g in G4:
                rw_v += ([f"X{s}{g}"] if s < 64 else []) + [f"Z{s}{g}"]
        rw_q = ["vb"]
        for d in range(2):
            rw_q += [f"{n}{d}" for n in ("rt", "zt")]
        rw_q += ["kbs"]
        for s in range(NCH):
            rw_p += [f"R{s}", f"SA{s}"] + ([f"S{s}"] if s < NCH - 1 else []) + [f"Y{s}"]
            rw_a += [f"R{s}"]
            rw_v += ([f"SD{s}"] if 0 < s < NCH - 1 else []) + [f"SA{s}"] + ([f"S{s}0", f"S{s}1"] if s < NCH - 1 else []) + ([f"SS{s}"] if 0 < s < NCH - 1 else [])
        rw_a += ["Yev"]
        rw_p += ["GM"]
        rw_v += ["yc"]
        rw_a += ["gsq"]
        rw_p += ["GV"]
        rw_a += ["gln", "grs"]
        rw_v += ["gn1", "gn2"]
        rw_q += ["gt"]
        rw_p, rw_a, rw_v, rw_q = steps("rw_p", rw_p), steps("rw_a", rw_a), steps("rw_v", rw_v), steps("rw_q", rw_q)
        up_p = steps("up_p", ["g0", "v0", "g1", "v1"])
        up_a = steps("up_a", ["cv0", "th0", "cv1", "th1"])
        up_v = steps("up_v", [f"{n}{q}" for q in range(2) for n in ("c1", "c2", "s", "a")])
        dnw_p = steps("dnw_p", ["w"])
        down_p = steps("down_p", [f"m{m}" for m in range(KD)])
        passed = {"sp": sem("sp_passed"), "pe": sem("pe_passed"), "dve": sem("dve_passed"), "pool": sem("pool_passed")}

        def settle(eng, name):
            eng.sem_inc(passed[name], 1)

        def credit(eng, mine):
            for s in mine:
                eng.sem_inc(s.sem, len(s.names))

        block = ctx.enter_context(nc.Block())

        @block.sync
        def _(sp):
            sp.dma_start(CST[:, :], cst).then_inc(const_in, 16)
            sp.dma_start(LEV_IN.bitcast(I32), lev).then_inc(const_in, 16)
            sp.dma_start(POS_IN.bitcast(I32), pos.partition_broadcast(P)).then_inc(pos_in, 16)
            sp.dma_start(CACT, c.partition_broadcast(P)).then_inc(c_in, 16)
            for j in range(16):
                sp.dma_start(ADA0[j], ada[0, j]).then_inc(ada0_in[j // 4], 16)
            sp.dma_start(X[:, :].rearrange("p (k t) -> p k t", k=KD), x).then_inc(x_in, 16)
            for s in range(3):
                sp.dma_start(ring[s], tiles[s]).then_inc(ring_in[s], 16)

            def load_tile(l, t):
                sp.wait_ge(tile_done.sem, l * NTILE + t + (3 + 1))
                sp.dma_start(ring[t % 3], tiles[l * NTILE + t + 3]).then_inc(ring_in[t % 3], 16)

            def load_ada(layer, j, pairs):
                sp.wait_ge(ada_done.sem, pairs * 2 + 2)
                settle(sp, "sp")
                for u in range(2):
                    sp.dma_start(ADA[u], ada[layer, j + u]).then_inc(ada_in[u], 16)

            with sp.Fori(0, DEPTH) as l:
                sp.wait_ge(up_v.sem, up_v.before("a1", l * (NF // 2)))
                sp.dma_start(PR[:, :], prm[l]).then_inc(prm_in, 16)
                load_ada(l, 16, l * 24 + 8)
                for t in range(7):
                    if t >= 5:
                        load_ada(l, 2 * t + 8, l * 24 + (t + 4))
                    load_tile(l, t)
                with sp.Fori(0, RB) as b:
                    for i in range(3):
                        load_ada(l, b * 6 + (22 + 2 * i), l * 24 + b * 3 + (11 + i))
                        sp.wait_ge(tile_done.sem, l * NTILE + b * 3 + (7 + i + 4))
                        sp.dma_start(ring[(7 + i) % 3], tiles[l * NTILE + b * 3 + (7 + i + 3)]).then_inc(
                            ring_in[(7 + i) % 3], 16)
                load_ada(l, 46, l * 24 + 23)
                with sp.Fori(0, HEADS // 2) as hp:
                    sp.wait_ge(att_p.sem, att_p.before("v1", l * 2 + hp))
                    sp.dma_start(MW, mlaw[l, hp]).then_inc(mla_in, 16)
                with sp.Fori(0, RB) as b:
                    sp.wait_ge(rw_p.sem, rw_p.before("G", l * RB + b))
                    sp.dma_start(l_dir, lora[l, b, :, 0:4]).then_inc(lora_in, 16)
                    sp.dma_start(l_gate[:, :], lora[l, b, :, 4]).then_inc(lora_in, 16)
                sp.wait_ge(rw_p.sem, rw_p.at("GV", l * RB + RB - 1))
                sp.wait_ge(rw_v.sem, rw_v.at("gn2", l * RB + RB - 1))
                sp.wait_ge(rw_q.sem, rw_q.at("gt", l * RB + RB - 1))
                for q in range(2):
                    sp.dma_start(MW_IN[q], mlp[l * NMLP + q]).then_inc(mlp_in[q], 16)
                load_ada(1 - l, 0, l * 24 + 24)
                for t in range(NPROJ, NTILE - 3):
                    load_tile(l, t)
                for t in range(NTILE - 3, NTILE):
                    load_tile(l, t)

                def load_mlp(u, q):
                    sp.dma_start(MW_IN[q], mlp[u]).then_inc(mlp_in[q], 16)

                def up_tiles(first, count, ada_too):
                    with sp.Fori(0, count) as i:
                        for q in range(2):
                            sp.wait_ge(up_p.sem, up_p.at(f"v{q}", l * (NF // 2) + i + first))
                            load_mlp(l * NMLP + i * 2 + (2 + q + 2 * first), q)
                            if ada_too and q == 0:
                                load_ada(1 - l, i * 2 + 2, l * 24 + i + 25)

                up_tiles(0, 7, True)
                up_tiles(7, NF // 2 - 7, False)
                with sp.Fori(0, NDN // 2 - 1) as i:
                    for q in range(2):
                        sp.wait_ge(dnw_p.sem, dnw_p.at("w", l * (NDN - 1) + i * 2 + q))
                        load_mlp(l * NMLP + i * 2 + (NUP + 2 + q), q)
                sp.wait_ge(dnw_p.sem, dnw_p.at("w", l * (NDN - 1) + NDN - 3))
                load_mlp(l * NMLP + NMLP - 1, 0)
            for s in range(3):
                sp.wait_ge(ring_in[s], 16 * (DEPTH * NTILE // 3 + 1))
            for u in range(2):
                sp.wait_ge(ada_in[u], 16 * 24 * DEPTH)
            for k in range(KD):
                sp.wait_ge(x_ready.sem, x_ready.at(f"x{k}", 2 * DEPTH + 1))
                sp.dma_start(out[k], xk(k)).then_inc(out_done, 16)
            sp.wait_ge(out_done, 16 * KD)

        @block.tensor
        def _(pe):
            credit(pe, [tile_done, nrm_p, sta_p, att_p, on_p, rw_p, up_p, dnw_p, down_p])
            mm = pe.matmul
            pe.wait_ge(const_in, 32)

            def mm3(out, w_hi, w_lo, x_hi, x_lo, start, stop):
                mm(out, w_hi, x_hi, start=start, stop=False)
                mm(out, w_hi, x_lo, start=False, stop=False)
                return mm(out, w_lo, x_hi, start=False, stop=stop)

            def norm_sums(n):
                for k in range(KD):
                    pe.wait_ge(nrm_a.sem, nrm_a.at(f"sq{k}", n))
                    mm(PS[7][:, :], ones, sq[k % 2], start=(k == 0), stop=(k == KD - 1)).then_inc(nrm_p.sem, nrm_p.one(f"sum{k}"))

            def project(l, t, bank, lo, free, part):
                pe.wait_ge(spl_q.sem, l * NTILE + t + (1 + 3))
                free()
                for k in range(KD):
                    part(k)
                    last = mm3(PS[bank][:, :], ring_h[t % 3][:, k, :], ring_l[t % 3][:, k, :], hhk(k), lo(k), k == 0, k == KD - 1)
                last.then_inc(tile_done.sem, tile_done.one(f"t{t % 3}"))

            with pe.Fori(0, DEPTH) as l:
                norm_sums(2 * l)
                for t in range(7):
                    project(l, t, t, hlk, lambda: None,
                            lambda k: pe.wait_ge(nrm_v.sem, nrm_v.at(f"l{k}", 2 * l)) if t == 0 else None)
                with pe.Fori(0, RB) as b:
                    for i in range(3):
                        t, bank = 7 + i, 4 + i
                        pe.wait_ge(spl_q.sem, l * NTILE + b * 3 + (t + 1 + 3))
                        pe.wait_ge(in_v.sem, in_v.at(("xw2", "xa2", "xg2")[i], l))
                        pe.wait_ge(rkv_v.sem, rkv_v.before(("r2", "k2", "v2")[i], l * RB + b))
                        for k in range(KD):
                            last = mm3(PS[bank][:, :], ring_h[t % 3][:, k, :], ring_l[t % 3][:, k, :], hhk(k), hlk(k), k == 0, k == KD - 1)
                        last.then_inc(tile_done.sem, tile_done.one(f"t{t % 3}"))
                pe.wait_ge(rkv_v.sem, rkv_v.at("v2", l * RB + RB - 1))
                for i in range(7):
                    pe.wait_ge(sta_a.sem, sta_a.at(f"sq{i}", l))
                    bank = (0, 0, 1, 2, 3, 4, 5)[i]
                    mm(PS[bank][:, :], ones if i < 3 else head_ones, sq[i % 2], start=(i != 1),
                       stop=(i != 0)).then_inc(sta_p.sem, sta_p.one(f"s{i}"))
                mm(PS[6][:, :], swap, RAW[:, 3, :], start=True, stop=True).then_inc(sta_p.sem, sta_p.one("perm"))
                with pe.Fori(0, HEADS // 2) as hp:
                    it = l * 2 + hp
                    wq = MW[:, 0:768].rearrange("p (c n) -> p c n", c=2)
                    wkv = MW[:, 768:1280]
                    pe.wait_ge(mla_in, (it + 1) * 16)
                    pe.wait_ge(sta_v.sem, sta_v.at("kvn", l))
                    pe.wait_ge(sta_a.sem, sta_a.at("ln5", l))
                    pe.wait_ge(att_v.sem, att_v.before("o1", it))
                    pe.wait_ge(att_a.sem, att_a.before("pt7", it))
                    for j, name in enumerate(("qA", "qB", "qp")):
                        for k in range(2):
                            last = mm(PS[j][:, :], wq[:, k, j * P:(j + 1) * P], LAT[:, k, :], start=(k == 0), stop=(k == 1))
                        last.then_inc(att_p.sem, att_p.one(name))
                    for j, name in enumerate(("kA", "kB")):
                        mm(PS[3 + j][:, :], wkv[:, j * P:(j + 1) * P], LAT[:, 2, :], start=True,
                           stop=True).then_inc(att_p.sem, att_p.one(name))
                    for j in range(2):
                        for u in range(2):
                            tb = 2 * j + u
                            last = mm(PS[5 + j][:, u * 256:(u + 1) * 256], LAT[:, 2, tb * P:(tb + 1) * P], wkv[:, 256:512],
                                      start=True, stop=True)
                        last.then_inc(att_p.sem, att_p.one(f"v{j}"))
                    pe.wait_ge(att_a.sem, att_a.at("qp", it))
                    mm(PS[7][:, :], swap, QPR, start=True, stop=True).then_inc(att_p.sem, att_p.one("perm"))
                    pe.wait_ge(att_v.sem, att_v.at("rp3", it))
                    pe.wait_ge(att_a.sem, att_a.at("qB", it))
                    for i in range(10):
                        if i < 8:
                            e, qb = divmod(i, 4)
                            bank = PS[(0, 1, 7)[i % 3]]
                            if i >= 3:
                                pe.wait_ge(att_a.sem, att_a.at(f"ex{i - 3}", it))
                            mm(bank[:, :], QN[:, e, qb * P:(qb + 1) * P], KN[:, e, :], start=True, stop=False)
                            mm(bank[:, :], QPE[:, qb * P:(qb + 1) * P], KPE[e], start=False,
                               stop=True).then_inc(att_p.sem, att_p.one(f"sc{i}"))
                        if i >= 2:
                            j = i - 2
                            pe.wait_ge(att_v.sem, att_v.at(f"pn{j}", it))
                            if j >= 2:
                                pe.wait_ge(att_a.sem, att_a.at(f"pt{j - 2}", it))
                            for kb in range(4):
                                last = pe.transpose(PS[2 + j % 2][:, kb * P:(kb + 1) * P], PB[j % 3][:, kb * P:(kb + 1) * P], ident)
                            last.then_inc(att_p.sem, att_p.one(f"tr{j}"))
                        if i in (6, 9):
                            e = i // 9
                            pe.wait_ge(att_a.sem, att_a.at(f"pt{4 * e + 3}", it))
                            for kb in range(4):
                                last = mm(PS[4 + e][:, :], VT_A[:, kb, e * P:(e + 1) * P], PTb[e][:, kb, :],
                                          start=(kb == 0), stop=(kb == 3))
                            last.then_inc(att_p.sem, att_p.one(f"pv{e}"))
                for i in range(4):
                    pe.wait_ge(on_a.sem, on_a.at(f"sq{i}", l))
                    mm(PS[6][:, :], ones, sq[i % 2], start=(i == 0), stop=(i == 3)).then_inc(on_p.sem, on_p.one(f"s{i}"))
                with pe.Fori(0, RB) as b:
                    it = l * RB + b
                    A, V, Q = (lambda n: pe.wait_ge(rw_a.sem, rw_a.at(n, it))), (lambda n: pe.wait_ge(rw_v.sem, rw_v.at(n, it))), (
                        lambda n: pe.wait_ge(rw_q.sem, rw_q.at(n, it)))

                    def done(ins, name):
                        ins.then_inc(rw_p.sem, rw_p.one(name))

                    pe.wait_ge(lora_in, (it + 1) * 32)
                    pe.wait_ge(on_a.sem, on_a.at("rs", l))
                    pe.wait_ge(rw_a.sem, rw_a.before("Yev", it))
                    pe.wait_ge(rw_v.sem, rw_v.before(f"SA{NCH - 1}", it))
                    for d in range(2):
                        done(mm(PS[2 * d][:, :], l_dir[:, d, :], mix(XW), start=True, stop=True), f"W{d}")
                        done(mm(PS[2 * d + 1][:, :], l_dir[:, 2 + d, :], mix(XA), start=True, stop=True), f"A{d}")
                    done(mm(PS[4][:, :], l_gate[:, :], mix(XG), start=True, stop=True), "G")
                    pe.wait_ge(rw_v.sem, rw_v.before("yc", it))
                    pe.wait_ge(rw_a.sem, rw_a.before("gln", it))
                    Q("vb")
                    for c4 in range(NCH):
                        last = pe.transpose(PS[5][:, c4 * P:(c4 + 1) * P], VB[:, c4 * P:(c4 + 1) * P], ident)
                    done(last, "VT")
                    for d in range(2):
                        for m, (src, last_v) in enumerate(((BH[d], f"bh1{d}"), (KH[d], f"kh1{d}"))):
                            V(last_v)
                            for e in range(2):
                                name = f"{('BT', 'KT')[m]}{d}{e}"
                                A({"BT00": "VT", "KT01": "gate"}.get(name, "VT") if d == 0 else name[:2] + f"0{e}")
                                for c4 in range(NCH):
                                    last = pe.transpose(PS[(5, 6, 7, 4)[2 * m + e]][:, c4 * P:(c4 + 1) * P],
                                                        src[e][:, c4 * P:(c4 + 1) * P], ident)
                                done(last, name)
                        Q(f"zt{d}")
                        A(f"A{d}")
                        if d == 0:
                            A("A1")
                        for g in (2 * d, 2 * d + 1):
                            for m, src in enumerate((BH[d][g % 2], KH[d][g % 2])):
                                for h in range(2):
                                    bank = 2 * m + h
                                    if g:
                                        V(f"{('Gb', 'Gk')[m]}{g - 1}{h}")
                                    for c4 in (2 * h, 2 * h + 1):
                                        last = mm(PS[bank][:, (c4 % 2) * 256:(c4 % 2) * 256 + 256],
                                                  src[:, c4 * P:(c4 + 1) * P], ZR[d][:, c4, :, :], start=True, stop=True)
                                    done(last, f"{('Gb', 'Gk')[m]}{g}{h}")
                    V("kbr")
                    A("KT11")
                    done(mm(PS[7][:, :], head_ones, LW, start=True, stop=True), "BON")
                    V("bon")
                    V("Gk31")
                    for g in G4:
                        for c4 in range(NCH):
                            last = pe.transpose(PS[2 * g + 1][:, c4 * P:(c4 + 1) * P], GB[g][:, c4, 0, :], ident)
                        done(last, f"LT{g}")
                    for j, s in enumerate(LEVELS[1:]):
                        for g in G4:
                            V(f"Z{LEVELS[j]}{g}")
                            for c4 in range(NCH):
                                last = mm(PS[2 * g][:, c4 * P:(c4 + 1) * P], GB[g][:, c4, 0, :], XX[g][:, c4, :], start=True, stop=True)
                            done(last, f"T{s}{g}")
                        for g in G4:
                            A(f"T{s}{g}")
                            if s < 64:
                                for c4 in range(NCH):
                                    last = mm(PS[2 * g + 1][:, c4 * P:(c4 + 1) * P], XT[g][:, c4, :], TT[g][:, c4, :], start=True, stop=True)
                                done(last, f"X{s}{g}")
                            for c4 in range(NCH):
                                last = mm(PS[2 * g][:, c4 * P:(c4 + 1) * P], TT[g][:, c4, :], XT[g][:, c4, :], start=True, stop=True)
                            done(last, f"Z{s}{g}")
                    V("Z643")
                    for s in range(NCH):
                        ch = (s, NCH - 1 - s)
                        rb = 0 if s % 2 == 0 else 4
                        for g in G4:
                            d = g // 2
                            last = mm(PS[rb][:, g * P:(g + 1) * P], GK[g][:, ch[d], 0, :], VT[:, ch[d], :],
                                      start=(g == 0), stop=(s == 0), skip_group_check=True)
                        if s:
                            V("S01" if s == 1 else f"SS{s - 1}")
                            for d in range(2):
                                last = mm(own(rb, d), ZR[d][:, ch[d], 0, :], SM[:, d, :], start=False, stop=True, skip_group_check=True)
                        done(last, f"R{s}")
                        for g in G4:
                            d, e = divmod(g, 2)
                            mm(PS[3][64 * e:64 * e + 64, ch[d] * P:(ch[d] + 1) * P], VT[:, ch[d], e * 64:(e + 1) * 64],
                               GK[g][:, ch[d], 1, :], start=(s == 0 and d == 0), stop=False, skip_group_check=True)
                        if s:
                            for d in range(2):
                                mm(PS[3][:, ch[d] * P:(ch[d] + 1) * P], SM[:, d, :], ZR[d][:, ch[d], 1, :], start=False, stop=False,
                                   skip_group_check=True)
                        A(f"R{s}")
                        if s:
                            V(f"SA{s - 1}")
                        for g in G4:
                            last = mm(PS[1][:, g * P:(g + 1) * P], XT[g][:, ch[g // 2], :], RHS[:, g // 2, :], start=True, stop=True)
                        done(last, f"SA{s}")
                        V(f"SA{s}")
                        if s < NCH - 1:
                            for d in range(2):
                                so = PS[2][:, d * P:(d + 1) * P]
                                mm(so, KT[d][:, ch[d], :], VT[:, ch[d], :], start=True, stop=False)
                                last = mm(so, BT[d][:, ch[d], :], SA[:, d, :], start=False, stop=True)
                            done(last, f"S{s}")
                        for g in G4:
                            d, e = divmod(g, 2)
                            last = mm(PS[3][64 * e:64 * e + 64, ch[d] * P:(ch[d] + 1) * P], SA[:, d, e * 64:(e + 1) * 64],
                                      GB[g][:, ch[d], 1, :], start=False, stop=(s == NCH - 1), skip_group_check=True)
                        done(last, f"Y{s}")
                    A("Yev")
                    done(mm(PS[5][:, :], head_ones, PP, start=True, stop=True), "GM")
                    A("gsq")
                    done(mm(PS[6][:, :], head_ones, sq[0], start=True, stop=True), "GV")
                for m in range(KD):
                    t = NPROJ + m

                    def free():
                        if m >= 4:
                            pe.wait_ge(x_ready.sem, x_ready.at(f"x{m - 4}", 2 * l + 1))
                    project(l, t, m % 4, ylk, free, lambda k: pe.wait_ge(y_v.sem, y_v.at(f"y{k}", l)) if m == 0 else None)
                norm_sums(2 * l + 1)
                with pe.Fori(0, NF // 2) as i:
                    it = l * (NF // 2) + i
                    for q in range(2):
                        pe.wait_ge(up_v.sem, up_v.before(f"a{q}", it))
                        for half, part in enumerate((msp_q, msp_v)):
                            pe.wait_ge(part.sem, part.at(f"l{half}", l * NMLP + i * 2 + q))
                            for k in range(KD):
                                if q == 0 and half == 0:
                                    pe.wait_ge(nrm_v.sem, nrm_v.at(f"l{k}", 2 * l + 1))
                                last = mm3(PS[2 * q + half][:, :], MW_H[q][:, half, k, :], MW_L[q][:, half, k, :], hhk(k), hlk(k),
                                           k == 0, k == KD - 1)
                            last.then_inc(up_p.sem, up_p.one(f"{'gv'[half]}{q}"))

                def down_tile(w, q, first, final):
                    for j, part in enumerate((msp_q, msp_v)):
                        pe.wait_ge(part.sem, part.at(f"l{j}", w + (l * NMLP + NUP)))
                        pe.wait_ge(act_v.sem, act_v.at(f"l{j}", w + l * NDN))
                        for m in range(KD):
                            if first and j == 0 and m == 4:
                                pe.wait_ge(up_v.sem, up_v.at("a1", (l + 1) * (NF // 2) - 1))
                            last = mm3(PS[DN_BANK[m]][:, :], MW_H[q][:, j, m, :], MW_L[q][:, j, m, :], ACT_H[q][:, j, :], act_lo(w, j),
                                       first and j == 0, final and j == 1)
                            if final and j == 1:
                                last.then_inc(down_p.sem, down_p.one(f"m{m}"))
                    if not final:
                        last.then_inc(dnw_p.sem, dnw_p.one("w"))

                act_lo = lambda w, j: MIX_R[:, bass.ds(w * (2 * SEQ) + j * SEQ, SEQ)]
                down_tile(0, 0, True, False)
                down_tile(1, 1, False, False)
                with pe.Fori(1, NDN // 2) as i:
                    for q in range(2):
                        down_tile(i * 2 + q, q, False, False)
                down_tile(NDN - 1, 0, False, True)
            norm_sums(2 * DEPTH)

        @block.scalar
        def _(act):
            credit(act, [pro_a, nrm_a, in_a, rkv_a, sta_a, att_a, on_a, rw_a, up_a, spl_a, y_a, msp_a, act_a])
            F = act.activation
            act.wait_ge(const_in, 32)
            act.wait_ge(pro_v.sem, pro_v.at("s16", 0))
            F(sin, sin, ACT.Sin).then_inc(pro_a.sem, pro_a.one("sin"))
            F(cos, cos, ACT.Sin).then_inc(pro_a.sem, pro_a.one("cos"))
            act.wait_ge(c_in, 16)
            F(TANH_C, CACT, ACT.Tanh, scale=0.5).then_inc(pro_a.sem, pro_a.one("tanh"))
            act.wait_ge(x_in, 16)

            def split_tile(l, t):
                act.wait_ge(ring_in[t % 3], (l * (NTILE // 3) + (t // 3 + 1)) * 16)
                F(ring_h[t % 3], ring[t % 3], ACT.Identity).then_inc(spl_a.sem, spl_a.one(f"t{t % 3}"))

            def split_mlp(l, pair, q):
                act.wait_ge(mlp_in[q], (l * (NMLP // 2 + 1 - q) + pair + 1) * 16)
                for half in range(2):
                    F(MW_H[q][:, half], MW_IN[q][:, half], ACT.Identity).then_inc(msp_a.sem, msp_a.one(f"h{half}"))

            def norm(n, h=True, between=lambda: None):
                for k in range(KD):
                    act.wait_ge(x_ready.sem, x_ready.at(f"x{k}", n))
                    if k >= 2:
                        act.wait_ge(nrm_p.sem, nrm_p.at(f"sum{k - 2}", n))
                    F(sq[k % 2], xk(k), ACT.Square).then_inc(nrm_a.sem, nrm_a.one(f"sq{k}"))
                between()
                act.wait_ge(nrm_p.sem, nrm_p.at(f"sum{KD - 1}", n))
                F(rs[0], PS[7][:, :], ACT.Ln, bias=k_eps, scale=1.0 / DM).then_inc(nrm_a.sem, nrm_a.one("ln"))
                act.wait_ge(nrm_a.sem, nrm_a.at("ln", n))
                F(rs[1], rs[0], ACT.Exp, scale=-0.5).then_inc(nrm_a.sem, nrm_a.one("rstd"))
                if h is False:
                    return
                for k in range(KD):
                    act.wait_ge(nrm_v.sem, nrm_v.at(f"t{k}", n))
                    F(hhk(k), hk(k), ACT.Identity, bias=MOD[:, h + k:h + k + 1]).then_inc(nrm_a.sem, nrm_a.one(f"h{k}"))

            def scaled(bank, dst, j):
                return F(dst, PS[bank][:, :], ACT.Identity, scale=col(DR, DRV["mu_c"] + j))

            with act.Fori(0, DEPTH) as l:
                for t in range(2):
                    split_tile(l, t)
                act.wait_ge(lay_v.sem, lay_v.at("muc", l))
                norm(2 * l, 0)
                for j in range(4):
                    split_tile(l, j + 2)
                    act.wait_ge(tile_done.sem, l * NTILE + (j + 1 + 3))
                    F(RAW[:, j, :], PS[j][:, :], ACT.Identity).then_inc(in_a.sem, in_a.one(f"raw{j}"))
                for j, name in enumerate(("xw", "xa", "xg")):
                    split_tile(l, j + 6)
                    act.wait_ge(tile_done.sem, l * NTILE + (4 + j + 1 + 3))
                    scaled(4 + j, mix((XW, XA, XG)[j]), j).then_inc(in_a.sem, in_a.one(name))
                    if j == 1:
                        act.wait_ge(in_v.sem, in_v.at("xw2", l))
                        F(mix(XW), mix(XW), ACT.Tanh).then_inc(in_a.sem, in_a.one("txw"))
                    if j == 2:
                        act.wait_ge(in_v.sem, in_v.at("xg2", l))
                        F(mix(XG), mix(XG), ACT.Tanh, scale=0.5).then_inc(in_a.sem, in_a.one("txg"))
                with act.Fori(0, RB) as b:
                    for i, name in enumerate("rkv"):
                        s = (9 + i) % 3
                        act.wait_ge(ring_in[s], (l * (NTILE // 3) + b + ((9 + i) // 3 + 1)) * 16)
                        F(ring_h[s], ring[s], ACT.Identity).then_inc(spl_a.sem, spl_a.one(f"t{s}"))
                        act.wait_ge(tile_done.sem, l * NTILE + b * 3 + (7 + i + 1 + 3))
                        scaled(4 + i, MIX[:, bass.ds(b * SEQ + 4 * i * SEQ, SEQ)], b * 3 + (3 + i)).then_inc(rkv_a.sem, rkv_a.one(name))
                for i in range(7):
                    if i >= 2:
                        act.wait_ge(sta_p.sem, sta_p.at(f"s{i - 2}", l))
                    if i < 3:
                        if i == 0:
                            act.wait_ge(in_a.sem, in_a.at("txg", l))
                        src = RAW[:, i, :]
                    else:
                        act.wait_ge(sta_v.sem, sta_v.at(f"kk{i - 3}", l))
                        src = mix(KK0 + i - 3)
                    F(sq[i % 2], src, ACT.Square).then_inc(sta_a.sem, sta_a.one(f"sq{i}"))
                for i in range(6):
                    act.wait_ge(sta_p.sem, sta_p.at(f"s{i + 1}", l))
                    F(LOGS[i], PS[i][:, :], ACT.Ln, bias=k_eps if i < 2 else k_kkeps,
                      scale=(1.0 / QR, 1.0 / KVR, 1, 1, 1, 1)[i]).then_inc(sta_a.sem, sta_a.one(f"ln{i}"))
                for i in range(6):
                    act.wait_ge(sta_a.sem, sta_a.at(f"ln{i}", l))
                    F(LOGS[i], LOGS[i], ACT.Exp, scale=-0.5).then_inc(sta_a.sem, sta_a.one(f"rs{i}"))
                with act.Fori(0, HEADS // 2) as hp:
                    it = l * 2 + hp
                    act.wait_ge(sta_v.sem, sta_v.at("kkn3", l))
                    act.wait_ge(att_p.sem, att_p.before("pv1", it))
                    for j, (name, dst) in enumerate((("qA", QN[:, 0, :]), ("qB", QN[:, 1, :]), ("qp", QPR))):
                        act.wait_ge(att_p.sem, att_p.at(name, it))
                        F(dst, PS[j][:, :], ACT.Identity, scale=SCALE).then_inc(att_a.sem, att_a.one(name))
                    for i in range(10):
                        if i < 8:
                            act.wait_ge(att_v.sem, att_v.at(f"nm{i}", it))
                            if i >= 3:
                                act.wait_ge(att_p.sem, att_p.at(f"tr{i - 3}", it))
                            F(PB[i % 3], PS[(0, 1, 7)[i % 3]][:, :], ACT.Exp, bias=nmax[:, i:i + 1],
                              accum_out=rsum[:, i:i + 1]).then_inc(att_a.sem, att_a.one(f"ex{i}"))
                        if i >= 2:
                            j = i - 2
                            e, qb = divmod(j, 4)
                            act.wait_ge(att_p.sem, att_p.at(f"tr{j}", it))
                            F(PTb[e][:, :, qb * P:(qb + 1) * P], PS[2 + j % 2][:, :].rearrange("p (a b) -> p a b", a=4),
                              ACT.Identity).then_inc(att_a.sem, att_a.one(f"pt{j}"))
                for i in range(4):
                    act.wait_ge(att_v.sem, att_v.at("o1", l * 2 + 1))
                    if i >= 2:
                        act.wait_ge(on_p.sem, on_p.at(f"s{i - 2}", l))
                    F(sq[i % 2], yk(i), ACT.Square).then_inc(on_a.sem, on_a.one(f"sq{i}"))
                act.wait_ge(on_p.sem, on_p.at("s3", l))
                F(rs[0], PS[6][:, :], ACT.Ln, bias=k_eps, scale=1.0 / (HEADS * VD)).then_inc(on_a.sem, on_a.one("ln"))
                act.wait_ge(on_a.sem, on_a.at("ln", l))
                F(rs[1], rs[0], ACT.Exp, scale=-0.5).then_inc(on_a.sem, on_a.one("rs"))
                with act.Fori(0, RB) as b:
                    it = l * RB + b
                    PEw = lambda n: act.wait_ge(rw_p.sem, rw_p.at(n, it))
                    V = lambda n: act.wait_ge(rw_v.sem, rw_v.at(n, it))
                    Q = lambda n: act.wait_ge(rw_q.sem, rw_q.at(n, it))
                    A = lambda n: act.wait_ge(rw_a.sem, rw_a.at(n, it))

                    def done(ins, name):
                        ins.then_inc(rw_a.sem, rw_a.one(name))

                    act.wait_ge(rw_p.sem, rw_p.before("GV", it))
                    act.wait_ge(on_v.sem, on_v.at("y3", l))
                    def tanhs(d):
                        PEw(f"W{d}")
                        done(F(LW, PS[2 * d][:, :], ACT.Tanh, bias=col(DR, b + (DRV["w0h"] + 4 * d)), scale=0.5), f"W{d}")
                        PEw(f"A{d}")
                        done(F(AA, PS[2 * d + 1][:, :], ACT.Tanh, bias=col(DR, b + (DRV["a0h"] + 4 * d)), scale=0.5), f"A{d}")

                    def exps(d):
                        V(f"cc{d}")
                        done(F(PI, CW, ACT.Exp, scale=-1.0), f"Pi{d}")
                        done(F(PP, CW, ACT.Exp), f"Pp{d}")
                        V(f"ce{d}")
                        done(F(LW, LW, ACT.Exp), f"Pe{d}")
                        V(f"em{d}")
                        done(F(EM[d][:, d:d + 3], EM[d][:, d:d + 3], ACT.Exp), f"em{d}")

                    def token_major(m, d):
                        for e in range(2):
                            name = f"{('BT', 'KT')[m]}{d}{e}"
                            PEw(name)
                            bank = PS[(5, 6, 7, 4)[2 * m + e]][:, :].rearrange("p (a b) -> p a b", a=NCH)
                            done(F((BT, KT)[m][d][:, :, e * 64:(e + 1) * 64], bank[:, :, e * 64:(e + 1) * 64], ACT.Identity), name)

                    tanhs(0)
                    act.wait_ge(rw_v.sem, rw_v.before("gn2", it))
                    act.wait_ge(rw_q.sem, rw_q.before("gt", it))
                    exps(0)
                    PEw("G")
                    done(F(mix(GATE), PS[4][:, :], ACT.Identity), "gate")
                    PEw("VT")
                    done(F(VT, PS[5][:, :].rearrange("p (a b) -> p a b", a=NCH), ACT.Identity), "VT")
                    token_major(0, 0)
                    V("kd0")
                    Q("zt0")
                    tanhs(1)
                    token_major(1, 0)
                    V("kh10")
                    Q("rt0")
                    exps(1)
                    token_major(0, 1)
                    token_major(1, 1)
                    PEw("BON")
                    Q("kbs")
                    for g in G4:
                        done(F(XX[g], ident.unsqueeze(1).to_broadcast([P, NCH, P]), ACT.Identity), f"XI{g}")
                    PEw("Gk31")
                    for j, s in enumerate(LEVELS[1:]):
                        for g in G4:
                            PEw(f"T{s}{g}")
                            if s > 2:
                                PEw(f"Z{LEVELS[j]}{g}")
                            done(F(TT[g], PS[2 * g][:, :].rearrange("p (a b) -> p a b", a=NCH), ACT.Identity), f"T{s}{g}")
                    for s in range(NCH):
                        PEw(f"R{s}")
                        if s:
                            PEw(f"SA{s - 1}")
                        done(F(RHS.rearrange("p d (e v) -> p d e v", e=2), own(0 if s % 2 == 0 else 4), ACT.Identity), f"R{s}")
                    PEw(f"Y{NCH - 1}")
                    done(F(PP, PS[3][:, :], ACT.Identity), "Yev")
                    V("yc")
                    done(F(sq[0], PP, ACT.Square), "gsq")
                    PEw("GV")
                    done(F(sq[1], PS[6][:, :], ACT.Ln, bias=k_gneps, scale=1.0 / 64), "gln")
                    A("gln")
                    done(F(sq[0], sq[1], ACT.Exp, scale=-0.5), "grs")
                act.wait_ge(rw_p.sem, rw_p.at("GV", l * RB + RB - 1))
                act.wait_ge(rw_v.sem, rw_v.at("gn2", l * RB + RB - 1))
                for k in range(KD):
                    if k == KD - 1:
                        act.wait_ge(rw_q.sem, rw_q.at("gt", l * RB + RB - 1))
                    F(hhk(k), yk(k), ACT.Identity).then_inc(y_a.sem, y_a.one(f"y{k}"))
                for t in range(NPROJ + 2, NTILE):
                    split_tile(l, t)

                def first_tile():
                    act.wait_ge(tile_done.sem, (l + 1) * NTILE + 3)
                    split_mlp(l, 0, 0)

                norm(2 * l + 1, 24, first_tile)
                with act.Fori(0, NF // 2) as i:
                    it = l * (NF // 2) + i
                    for q in range(2):
                        if q == 0:
                            split_mlp(l, i, 1)
                        else:
                            split_mlp(l, i + 1, 0)
                        act.wait_ge(up_p.sem, up_p.at(f"g{q}", it))
                        act.wait_ge(up_v.sem, up_v.before(f"s{q}", it))
                        F(CV[q], PS[2 * q][:, :], ACT.Identity, bias=col(PR, i * 2 + (PRM["conv_b"] + q)),
                          scale=col(PR, i * 2 + (PRM["conv_w"] + NF + q))).then_inc(up_a.sem, up_a.one(f"cv{q}"))
                        act.wait_ge(up_v.sem, up_v.at(f"c2{q}", it))
                        act.wait_ge(up_v.sem, up_v.before(f"a{q}", it))
                        F(TH[q], CV[q], ACT.Tanh, scale=0.5).then_inc(up_a.sem, up_a.one(f"th{q}"))

                def split_acts(w, q):
                    for j in range(2):
                        F(ACT_H[q][:, j, :], MIX[:, bass.ds(w * (2 * SEQ) + j * SEQ, SEQ)], ACT.Identity).then_inc(
                            act_a.sem, act_a.one(f"h{j}"))

                act.wait_ge(up_v.sem, up_v.at("a1", l * (NF // 2) + 1))
                for w in range(2):
                    split_acts(w, w)
                split_mlp(l, NUP // 2, 1)
                act.wait_ge(up_v.sem, up_v.at("a1", (l + 1) * (NF // 2) - 1))
                with act.Fori(1, NDN // 2) as i:
                    for q in range(2):
                        act.wait_ge(dnw_p.sem, dnw_p.at("w", l * (NDN - 1) + i * 2 + (q - 2)))
                        split_acts(i * 2 + q, q)
                        split_mlp(l, i + NUP // 2, q)
                act.wait_ge(dnw_p.sem, dnw_p.at("w", l * (NDN - 1) + NDN - 3))
                split_acts(NDN - 1, 0)
                split_mlp(l, (NMLP - 1) // 2, 0)
            norm(2 * DEPTH, False)

        @block.vector
        def _(dve):
            credit(dve, [x_ready, ada_done, pro_v, nrm_v, lay_v, in_v, rkv_v, sta_v, att_v, on_v, rw_v, up_v, y_v, msp_v, act_v])
            TSC, TTT, STT = dve.tensor_scalar, dve.tensor_tensor, dve.scalar_tensor_tensor
            dve.wait_ge(const_in, 32)
            dve.wait_ge(pos_in, 16)
            two_pi = 2 * np.pi
            p1 = 6.28125
            p2 = float(np.round((two_pi - p1) * 2 ** 21) / 2 ** 21)
            p3 = float(two_pi - p1 - p2)
            turn, magic, limit = float(1 / two_pi), 1.5 * 2 ** 23, 3.1415925
            n = [0]

            def pro(ins):
                ins.then_inc(pro_v.sem, pro_v.one(f"s{n[0]}"))
                dve.wait_ge(pro_v.sem, pro_v.at(f"s{n[0]}", 0))
                n[0] += 1

            ang, rnd = RS[:, 0:SEQ], RS[:, SEQ:2 * SEQ]
            pro(dve.tensor_copy(LEV[:, :], LEV_IN.bitcast(I32)))
            pro(dve.tensor_copy(ang, POS_IN.bitcast(I32)))
            pro(TSC(ang, ang, CST[:, K_FREQ:K_FREQ + 1], None, ALU.mult))
            for dst, quarter in ((sin, 0.0), (cos, 0.25)):
                pro(TSC(rnd, ang, turn, quarter, ALU.mult, ALU.add))
                pro(TSC(rnd, rnd, magic, None, ALU.add))
                pro(TSC(rnd, rnd, magic, None, ALU.subtract))
                pro(STT(dst, rnd, -p1, ang, ALU.mult, ALU.add))
                pro(STT(dst, rnd, -p2, dst, ALU.mult, ALU.add))
                pro(STT(dst, rnd, -p3, dst, ALU.mult, ALU.add))
                if quarter:
                    TSC(dst, dst, float(np.pi / 2), limit, ALU.add, ALU.min).then_inc(pro_v.sem, pro_v.one("s15"))
                    dve.wait_ge(pro_v.sem, pro_v.at("s15", 0))
                    TSC(dst, dst, -limit, None, ALU.max).then_inc(pro_v.sem, pro_v.one("s16"))
                else:
                    TSC(dst, dst, limit, -limit, ALU.min, ALU.max)
                    n_ = n[0]
                    assert n_ == 9
            dve.wait_ge(pro_a.sem, pro_a.at("tanh", 0))
            TSC(sin, sin, CST[:, K_SIGN:K_SIGN + 1], None, ALU.mult)
            STT(CACT, TANH_C, 1.0, CACT, ALU.add, ALU.mult).then_inc(cact_done, 1)
            dve.wait_ge(cact_done, 1)

            def ada_cols(j, rnd, slots=ADA):
                if not (isinstance(rnd, int) and rnd == 0):
                    dve.wait_ge(mod_kept, rnd)
                for u in range(2):
                    if slots is ADA:
                        dve.wait_ge(ada_in[u], (rnd - 7) * 16)
                    dve.tensor_tensor_reduce(out=slots[u], in0=slots[u], in1=CACT, scale=0.5, scalar=0.0, op0=ALU.mult,
                                             op1=ALU.add, accum_out=dots[:, u:u + 1]).then_inc(ada_done.sem, ada_done.one(f"a{u}"))
                dve.wait_ge(ada_done.sem, ada_done.at("a1", rnd))
                dve.tensor_copy(MODR[:, bass.ds(j, 2)] if not isinstance(j, int) else MODR[:, j:j + 2], dots[:, :]).then_inc(
                    mod_kept, 1)

            for j in range(8):
                if j % 2 == 0:
                    dve.wait_ge(ada0_in[j // 2], 64)
                ada_cols(2 * j, j, ADA0[2 * j:2 * j + 2])
            dve.wait_ge(x_in, 16)
            dve.sem_inc(x_ready.sem, KD)
            x_ready.turn += KD

            def norm_rows(n, sc, sh):
                def rest(k):
                    dve.wait_ge(nrm_a.sem, nrm_a.at(f"h{k}", n))
                    STT(hlk(k), hk(k), MOD[:, sh + k:sh + k + 1], plain(hhk(k)), ALU.add, ALU.subtract).then_inc(
                        nrm_v.sem, nrm_v.one(f"l{k}"))

                dve.wait_ge(nrm_a.sem, nrm_a.at("rstd", n))
                for k in range(KD):
                    STT(hk(k), xk(k), MOD[:, sc + k:sc + k + 1], rs[1], ALU.mult, ALU.mult).then_inc(nrm_v.sem, nrm_v.one(f"t{k}"))
                    if k:
                        rest(k - 1)
                rest(KD - 1)

            def rest_mlp(l, u, q):
                dve.wait_ge(msp_a.sem, msp_a.at("h1", l * NMLP + u))
                TTT(MW_L[q][:, 1], MW_IN[q][:, 1], plain(MW_H[q][:, 1]), ALU.subtract).then_inc(msp_v.sem, msp_v.one("l1"))

            def shift(bank, dst, j, s, a, b, rnd):
                STT(dst[:, 1:SEQ], PS[bank][:, 0:SEQ - 1], col(PR, j + PRM["mu0"]), dst[:, 1:SEQ], ALU.mult, ALU.add).then_inc(s.sem, s.one(a))
                dve.wait_ge(s.sem, s.at(a, rnd))
                return STT(dst[:, 0:SEQ - 1], PS[bank][:, 1:SEQ], col(PR, j + PRM["mu1"]), dst[:, 0:SEQ - 1], ALU.mult, ALU.add)

            with dve.Fori(0, DEPTH) as l:
                dve.wait_ge(prm_in, (l + 1) * 16)
                dve.wait_ge(mod_kept, l * 24 + 8)

                def lay(ins, name):
                    ins.then_inc(lay_v.sem, lay_v.one(name))
                    dve.wait_ge(lay_v.sem, lay_v.at(name, l))

                pcol = lambda n, w: PR[:, PRM[n]:PRM[n] + w]
                dcol = lambda n, w: DR[:, DRV[n]:DRV[n] + w]
                lay(TTT(MOD[:, 0:16], MODR[:, 0:16], PR[:, 0:16], ALU.add), "modA")
                lay(TSC(MOD[:, 8:16], MOD[:, 8:16], 1.0, None, ALU.add), "modA1")
                lay(TSC(dcol("w0h", 16), pcol("w0", 16), 0.5, None, ALU.mult), "w0h")
                lay(TSC(dcol("ka_h", 4), pcol("k_a", 4), 0.5, None, ALU.mult), "kah")
                lay(TSC(dcol("ka_c", 4), pcol("k_a", 4), -0.5, 1.0, ALU.mult, ALU.add), "kac")
                lay(TSC(dcol("r_kh", 4), pcol("r_k", 4), 0.5, None, ALU.mult), "rkh")
                lay(TTT(dcol("mu_c", 15), pcol("mu0", 15), pcol("mu1", 15), ALU.add), "mu01")
                lay(TSC(dcol("mu_c", 15), dcol("mu_c", 15), -1.0, 1.0, ALU.mult, ALU.add), "muc")
                norm_rows(2 * l, 8, 0)
                for j, name in enumerate(("xw", "xa", "xg")):
                    dve.wait_ge(in_a.sem, in_a.at(name, l))
                    shift(4 + j, mix((XW, XA, XG)[j]), j, in_v, f"{name}1", f"{name}2", l).then_inc(in_v.sem, in_v.one(f"{name}2"))
                    ada_cols(16 + 2 * j, l * 24 + (8 + j))
                dve.wait_ge(in_a.sem, in_a.at("txg", l))
                TSC(mix(XG), mix(XG), 1.0, 0.5, ALU.add, ALU.mult).then_inc(in_v.sem, in_v.one("sxg"))
                with dve.Fori(0, RB) as b:
                    for i, name in enumerate("rkv"):
                        dve.wait_ge(rkv_a.sem, rkv_a.at(name, l * RB + b))
                        shift(4 + i, MIX[:, bass.ds(b * SEQ + 4 * i * SEQ, SEQ)], b * 3 + (3 + i), rkv_v, f"{name}1", f"{name}2",
                              l * RB + b).then_inc(rkv_v.sem, rkv_v.one(f"{name}2"))
                        ada_cols(b * 6 + (22 + 2 * i), l * 24 + b * 3 + (11 + i))
                ada_cols(46, l * 24 + 23)
                dve.wait_ge(mod_kept, l * 24 + 24)
                lay(TTT(MOD[:, 16:48], MODR[:, 16:48], PR[:, 16:48], ALU.add), "modB")
                lay(TSC(MOD[:, 32:40], MOD[:, 32:40], 1.0, None, ALU.add), "modB1")
                dve.wait_ge(rkv_v.sem, rkv_v.at("v2", l * RB + RB - 1))
                for b in range(RB):
                    TSC(mix(KK0 + b), mix(K0 + b), PR[:, PRM["k_k"] + b:PRM["k_k"] + b + 1], None, ALU.mult).then_inc(
                        sta_v.sem, sta_v.one(f"kk{b}"))
                dve.wait_ge(sta_p.sem, sta_p.at("perm", l))
                TTT(KT1, RAW[:, 3, :], cos, ALU.mult).then_inc(sta_v.sem, sta_v.one("kp1"))
                TTT(KT2, PS[6][:, :], sin, ALU.mult).then_inc(sta_v.sem, sta_v.one("kp2"))
                dve.wait_ge(sta_v.sem, sta_v.at("kp2", l))
                TTT(KT1, KT1, KT2, ALU.add).then_inc(sta_v.sem, sta_v.one("kp3"))
                dve.wait_ge(sta_v.sem, sta_v.at("kp3", l))
                for e in range(2):
                    TSC(KPE[e], KT1, head[e], None, ALU.mult).then_inc(sta_v.sem, sta_v.one(f"kpm{e}"))
                dve.wait_ge(sta_a.sem, sta_a.at("rs0", l))
                for k in range(2):
                    STT(LAT[:, k, :], RAW[:, k, :], PR[:, PRM["q_gain"] + k:PRM["q_gain"] + k + 1], LOGS[0], ALU.mult, ALU.mult).then_inc(
                        sta_v.sem, sta_v.one(f"qn{k}"))
                dve.wait_ge(sta_a.sem, sta_a.at("rs1", l))
                STT(LAT[:, 2, :], RAW[:, 2, :], PR[:, PRM["kv_gain"]:PRM["kv_gain"] + 1], LOGS[1], ALU.mult, ALU.mult).then_inc(
                    sta_v.sem, sta_v.one("kvn"))
                for b in range(RB):
                    dve.wait_ge(sta_a.sem, sta_a.at(f"rs{2 + b}", l))
                    TTT(mix(KK0 + b), mix(KK0 + b), LOGS[2 + b], ALU.mult).then_inc(sta_v.sem, sta_v.one(f"kkn{b}"))
                with dve.Fori(0, HEADS // 2) as hp:
                    it = l * 2 + hp
                    dve.wait_ge(sta_v.sem, sta_v.at("kkn3", l))
                    for j, name in enumerate(("kA", "kB")):
                        dve.wait_ge(att_p.sem, att_p.at(name, it))
                        dve.tensor_copy(KN[:, j, :], PS[3 + j][:, :]).then_inc(att_v.sem, att_v.one(name))
                    for j in range(2):
                        dve.wait_ge(att_p.sem, att_p.at(f"v{j}", it))
                        dve.tensor_copy(VT_A[:, 2 * j:2 * j + 2, :], PS[5 + j][:, :].rearrange("p (a b) -> p a b", a=2)).then_inc(
                            att_v.sem, att_v.one(f"v{j}"))
                    dve.wait_ge(att_p.sem, att_p.at("perm", it))
                    dve.wait_ge(att_a.sem, att_a.at("qp", it))
                    TTT(KT1, QPR, cos, ALU.mult).then_inc(att_v.sem, att_v.one("rp1"))
                    TTT(KT2, PS[7][:, :], sin, ALU.mult).then_inc(att_v.sem, att_v.one("rp2"))
                    dve.wait_ge(att_v.sem, att_v.at("rp2", it))
                    TTT(QPE, KT1, KT2, ALU.add).then_inc(att_v.sem, att_v.one("rp3"))
                    for i in range(10):
                        if i < 8:
                            dve.wait_ge(att_p.sem, att_p.at(f"sc{i}", it))
                            dve.tensor_reduce(nmax[:, i:i + 1], PS[(0, 1, 7)[i % 3]][:, :], AX.X, ALU.max).then_inc(
                                att_v.sem, att_v.one(f"mx{i}"))
                            dve.wait_ge(att_v.sem, att_v.at(f"mx{i}", it))
                            TSC(nmax[:, i:i + 1], nmax[:, i:i + 1], -1.0, None, ALU.mult).then_inc(att_v.sem, att_v.one(f"nm{i}"))
                        if 1 <= i < 9:
                            j = i - 1
                            dve.wait_ge(att_a.sem, att_a.at(f"ex{j}", it))
                            dve.reciprocal(rsum[:, j:i], rsum[:, j:i]).then_inc(att_v.sem, att_v.one(f"rc{j}"))
                            dve.wait_ge(att_v.sem, att_v.at(f"rc{j}", it))
                            TSC(PB[j % 3], PB[j % 3], rsum[:, j:i], None, ALU.mult).then_inc(att_v.sem, att_v.one(f"pn{j}"))
                        if i in (7, 9):
                            e = i // 9
                            dve.wait_ge(att_p.sem, att_p.at(f"pv{e}", it))
                            dve.tensor_copy(Y[:, bass.ds(hp * (2 * SEQ) + e * SEQ, SEQ)], PS[4 + e][:, :]).then_inc(
                                att_v.sem, att_v.one(f"o{e}"))
                dve.wait_ge(on_a.sem, on_a.at("rs", l))
                for i in range(4):
                    STT(yk(i), yk(i), PR[:, PRM["out_gain"] + i:PRM["out_gain"] + i + 1], rs[1], ALU.mult, ALU.mult).then_inc(
                        on_v.sem, on_v.one(f"y{i}"))
                with dve.Fori(0, RB) as b:
                    it = l * RB + b
                    PEw = lambda n: dve.wait_ge(rw_p.sem, rw_p.at(n, it))
                    A = lambda n: dve.wait_ge(rw_a.sem, rw_a.at(n, it))
                    Q = lambda n: dve.wait_ge(rw_q.sem, rw_q.at(n, it))
                    V = lambda n: dve.wait_ge(rw_v.sem, rw_v.at(n, it))

                    def done(ins, name):
                        ins.then_inc(rw_v.sem, rw_v.one(name))

                    kk_b = at(MIX, b + KK0)
                    for d in range(2):
                        A(f"W{d}")
                        done(TSC(LW, LW, 1.0, DECAY / 2, ALU.add, ALU.mult), f"lw{d}")
                        V(f"lw{d}")
                        if d:
                            A("Pp0")
                            V("em0")
                        if d == 0:
                            done(dve.tensor_tensor_scan(CW, scan_mask, LW, 0.0, ALU.mult, ALU.add), "cw0")
                        else:
                            done(dve.tensor_tensor_scan(CW[:, ::-1], scan_mask, LW[:, ::-1], 0.0, ALU.mult, ALU.add), "cw1")
                        V(f"cw{d}")
                        cw4 = CW.rearrange("p (c t) -> p c t", c=NCH)
                        mid, end = (63, 127) if d == 0 else (64, 0)
                        done(dve.tensor_copy(MID[d], cw4[:, :, mid]), f"mid{d}")
                        V(f"mid{d}")
                        done(TTT(cw4, cw4, MID[d].unsqueeze(2).to_broadcast([P, NCH, C]), ALU.subtract), f"cc{d}")
                        V(f"cc{d}")
                        done(TTT(LW, CW, LW, ALU.subtract), f"ce{d}")
                        if d == 0:
                            done(TTT(EM[0][:, 0:3], cw4[:, 0:3, end], MID[0][:, 1:4], ALU.add), "em0")
                        else:
                            done(TTT(EM[1][:, 1:4], cw4[:, 1:4, end], MID[1][:, 0:3], ALU.add), "em1")
                        A(f"A{d}")
                        done(STT(BB, AA, 1.0, kk_b, ALU.add, ALU.mult), f"b1{d}")
                        V(f"b1{d}")
                        A(f"Pi{d}")
                        for e in range(2):
                            done(STT(BH[d][e], BB, nhead[e], PI, ALU.mult, ALU.mult), f"bh{e}{d}")
                        done(TSC(AA, AA, col(DR, b + DRV["ka_h"]), col(DR, b + DRV["ka_c"]), ALU.mult, ALU.add), f"f{d}")
                        V(f"f{d}")
                        done(TTT(KDD[d], at(MIX, b + K0), AA, ALU.mult), f"kd{d}")
                        V(f"kd{d}")
                        for e in range(2):
                            done(STT(KH[d][e], KDD[d], head[e], PI, ALU.mult, ALU.mult), f"kh{e}{d}")
                    for g in G4:
                        for m, dst in enumerate((GB[g], GK[g])):
                            for h in range(2):
                                name = f"{('Gb', 'Gk')[m]}{g}{h}"
                                PEw(name)
                                done(TTT(dst[:, 2 * h:2 * h + 2, :, :].rearrange("p a b c -> p a (b c)"),
                                         PS[2 * m + h][:, :].rearrange("p (a b) -> p a b", a=2),
                                         gmask[g // 2].unsqueeze(1).to_broadcast([P, 2, 256]), ALU.mult), name)
                    Q("kbs")
                    done(STT(LW, KDD[0], col(DR, b + DRV["r_kh"]), at(MIX, b + R0), ALU.mult, ALU.mult), "kbr")
                    PEw("BON")
                    done(TTT(mix(BON), PS[7][:, :], VB, ALU.mult), "bon")
                    for g in G4:
                        done(dve.tensor_copy(XT[g], ident.unsqueeze(1).to_broadcast([P, NCH, P])), f"ZI{g}")
                    V("ZI3")
                    for g in G4:
                        PEw(f"LT{g}")
                        A(f"XI{g}")
                        settle(dve, "dve")
                        done(dve.copy_predicated(XX[g], level_mask(1, g // 2, False), PS[2 * g + 1][:, :].rearrange("p (a b) -> p a b", a=NCH)), f"X1{g}")
                        done(dve.copy_predicated(XT[g], level_mask(1, g // 2, True), GB[g][:, :, 0, :]), f"Z1{g}")
                    for s in LEVELS[1:]:
                        for g in G4:
                            if s < 64:
                                PEw(f"X{s}{g}")
                                settle(dve, "dve")
                                done(dve.copy_predicated(XX[g], level_mask(s, g // 2, False), PS[2 * g + 1][:, :].rearrange("p (a b) -> p a b", a=NCH)), f"X{s}{g}")
                            PEw(f"Z{s}{g}")
                            settle(dve, "dve")
                            done(dve.copy_predicated(XT[g], level_mask(s, g // 2, True), PS[2 * g][:, :].rearrange("p (a b) -> p a b", a=NCH)), f"Z{s}{g}")
                    for s in range(NCH):
                        ch = (s, NCH - 1 - s)
                        if 0 < s < NCH - 1:
                            for d in range(2):
                                last = TSC(SMD[:, d, :], SM[:, d, :], EM[d][:, ch[d]:ch[d] + 1], None, ALU.mult)
                            done(last, f"SD{s}")
                        PEw(f"SA{s}")
                        if s:
                            PEw(f"Y{s - 1}")
                        done(dve.tensor_copy(SA.rearrange("p d (e v) -> p d e v", e=2), own(1)), f"SA{s}")
                        if s < NCH - 1:
                            PEw(f"S{s}")
                            for d in range(2):
                                if s == 0:
                                    A(f"em{d}")
                                done(STT(SM[:, d, :], PS[2][:, d * P:(d + 1) * P], EM[d][:, ch[d]:ch[d] + 1], head_ones, ALU.mult,
                                         ALU.mult), f"S{s}{d}")
                            V(f"S{s}1")
                            if s:
                                done(TTT(SM, SM, SMD, ALU.add), f"SS{s}")
                                V(f"SS{s}")
                    PEw("GM")
                    done(STT(PP, PS[5][:, :], -1.0 / 64, PP, ALU.mult, ALU.add), "yc")
                    A("grs")
                    done(STT(PP, PP, col(PR, b + PRM["gn_g"]), sq[0], ALU.mult, ALU.mult), "gn1")
                    V("gn1")
                    done(STT(PP, PP, col(PR, b + PRM["gn_b"]), mix(BON), ALU.add, ALU.add), "gn2")
                for k in range(KD):
                    dve.wait_ge(y_a.sem, y_a.at(f"y{k}", l))
                    TTT(ylk(k), yk(k), plain(hhk(k)), ALU.subtract).then_inc(y_v.sem, y_v.one(f"y{k}"))
                for m in range(KD):
                    dve.wait_ge(tile_done.sem, l * NTILE + (NPROJ + m + 1 + 3))
                    STT(xk(m), PS[m % 4][:, :], MOD[:, 16 + m:17 + m], xk(m), ALU.mult, ALU.add).then_inc(x_ready.sem, x_ready.one(f"x{m}"))
                norm_rows(2 * l + 1, 32, 24)
                rest_mlp(l, 0, 0)

                def up_tiles(first, count, ada_too):
                    with dve.Fori(0, count) as i:
                        it = l * (NF // 2) + i + first
                        for q in range(2):
                            rest_mlp(l, i * 2 + (2 * first + q + 1), 1 - q)
                            dve.wait_ge(up_a.sem, up_a.at(f"cv{q}", it))
                            STT(CV[q][:, 1:SEQ], PS[2 * q][:, 0:SEQ - 1], col(PR, i * 2 + (PRM["conv_w"] + 2 * first + q)),
                                CV[q][:, 1:SEQ], ALU.mult, ALU.add).then_inc(up_v.sem, up_v.one(f"c1{q}"))
                            dve.wait_ge(up_v.sem, up_v.at(f"c1{q}", it))
                            STT(CV[q][:, 0:SEQ - 1], PS[2 * q][:, 1:SEQ], col(PR, i * 2 + (PRM["conv_w"] + 2 * NF + 2 * first + q)),
                                CV[q][:, 0:SEQ - 1], ALU.mult, ALU.add).then_inc(up_v.sem, up_v.one(f"c2{q}"))
                            if ada_too and q == 0:
                                ada_cols(i * 2, l * 24 + i + 24)
                            dve.wait_ge(up_a.sem, up_a.at(f"th{q}", it))
                            STT(TH[q], TH[q], 1.0, CV[q], ALU.add, ALU.mult).then_inc(up_v.sem, up_v.one(f"s{q}"))
                            dve.wait_ge(up_v.sem, up_v.at(f"s{q}", it))
                            dve.wait_ge(up_p.sem, up_p.at(f"v{q}", it))
                            STT(MIX[:, bass.ds(i * (2 * SEQ) + (2 * first + q) * SEQ, SEQ)], PS[2 * q + 1][:, :], 0.5, TH[q], ALU.mult,
                                ALU.mult).then_inc(up_v.sem, up_v.one(f"a{q}"))

                up_tiles(0, 8, True)
                up_tiles(8, NF // 2 - 8, False)

                def rest_acts(w, q):
                    for j in range(2):
                        block, rest = (t[:, bass.ds(w * (2 * SEQ) + j * SEQ, SEQ)] for t in (MIX, MIX_R))
                        dve.wait_ge(act_a.sem, act_a.at(f"h{j}", l * NDN + w))
                        TTT(rest, block, plain(ACT_H[q][:, j, :]), ALU.subtract).then_inc(act_v.sem, act_v.one(f"l{j}"))

                rest_acts(0, 0)
                rest_acts(1, 1)
                rest_mlp(l, NUP + 1, 1)
                with dve.Fori(1, NDN // 2) as i:
                    for q in range(2):
                        rest_acts(i * 2 + q, q)
                        rest_mlp(l, i * 2 + (NUP + q), q)
                rest_acts(NDN - 1, 0)
                rest_mlp(l, NMLP - 1, 0)
                for m in range(KD):
                    dve.wait_ge(down_p.sem, down_p.at(f"m{m}", l))
                    STT(xk(m), PS[DN_BANK[m]][:, :], MOD[:, 40 + m:41 + m], xk(m), ALU.mult, ALU.add).then_inc(
                        x_ready.sem, x_ready.one(f"x{m}"))
            dve.wait_ge(nrm_a.sem, nrm_a.at("rstd", 2 * DEPTH))
            for k in range(KD):
                STT(xk(k), xk(k), CST[:, K_GAIN + k:K_GAIN + k + 1], rs[1], ALU.mult, ALU.mult).then_inc(
                    x_ready.sem, x_ready.one(f"x{k}"))

        @block.gpsimd
        def _(pool):
            credit(pool, [rw_q, spl_q, msp_q])

            def rest_tile(t, n):
                s = t % 3
                pool.wait_ge(spl_a.sem, n + (1 + 3))
                pool.tensor_tensor(ring_l[s], ring[s], plain(ring_h[s]), ALU.subtract).then_inc(spl_q.sem, spl_q.one(f"t{s}"))

            def rest_mlp(n, q):
                pool.wait_ge(msp_a.sem, msp_a.at("h0", n))
                pool.tensor_tensor(MW_L[q][:, 0], MW_IN[q][:, 0], plain(MW_H[q][:, 0]), ALU.subtract).then_inc(
                    msp_q.sem, msp_q.one("l0"))

            with pool.Fori(0, DEPTH) as l:
                with pool.Fori(0, (NPROJ + 2) // 3) as i:
                    for t in range(3):
                        rest_tile(t, l * NTILE + i * 3 + t)
                pool.wait_ge(att_p.sem, att_p.at("pv1", l * 2 + 1))
                settle(pool, "pool")
                with pool.Fori(0, RB) as b:
                    it = l * RB + b
                    PEw = lambda n: (pool.wait_ge(rw_p.sem, rw_p.at(n, it)), settle(pool, "pool"))
                    A = lambda n: (pool.wait_ge(rw_a.sem, rw_a.at(n, it)), settle(pool, "pool"))
                    V = lambda n: (pool.wait_ge(rw_v.sem, rw_v.at(n, it)), settle(pool, "pool"))
                    Q = lambda n: (pool.wait_ge(rw_q.sem, rw_q.at(n, it)), settle(pool, "pool"))
                    TTT = pool.tensor_tensor

                    def done(ins, name):
                        ins.then_inc(rw_q.sem, rw_q.one(name))

                    pool.wait_ge(rw_p.sem, rw_p.before("GV", it))
                    pool.wait_ge(rw_v.sem, rw_v.before("gn2", it))
                    settle(pool, "pool")
                    done(pool.tensor_copy(VB, at(MIX, b + V0)), "vb")
                    for d in range(2):
                        half = lambda z: ZR[d][:, :, z, :]
                        v4 = lambda ap: ap.rearrange("p (c t) -> p c t", c=NCH)
                        A(f"Pp{d}")
                        done(TTT(half(1), v4(at(MIX, b + R0)), v4(PP), ALU.mult), f"rt{d}")
                        A(f"Pe{d}")
                        done(TTT(half(0), v4(at(MIX, b + KK0)), v4(LW), ALU.mult), f"zt{d}")
                    V("kh11")
                    done(TTT(KDD[0], KDD[0], KDD[1], ALU.add), "kbs")
                    V("gn2")
                    done(TTT(at(Y, b + 4), PP, mix(GATE), ALU.mult), "gt")
                for t in range(NPROJ + 2, NTILE):
                    rest_tile(t, l * NTILE + t)
                rest_mlp(l * NMLP, 0)
                with pool.Fori(0, NMLP // 2) as i:
                    for q in range(2):
                        rest_mlp(l * NMLP + i * 2 + (1 + q), 1 - q)


def _blocks(w, starts, width=P):
    rows = w.shape[0]
    return np.stack([w[:, s:s + width].reshape(rows // P, P, width).transpose(1, 0, 2) for s in starts])


def _columns(v):
    return np.ascontiguousarray(v.reshape(-1, P).T)


def _constants():
    cst = np.zeros((P, NCST), np.float32)
    i = np.arange(P)
    cst[:, K_ID:K_ID + P] = np.eye(P)
    cst[:, K_ONE:K_ONE + P] = 1
    cst[:, K_BD:K_BD + P] = i[:, None] // 64 == i[None, :] // 64
    cst[i, K_SWAP + (i ^ 32)] = 1
    for d, (strict, incl) in enumerate(((i[None] > i[:, None], i[None] >= i[:, None]),
                                        (i[None] < i[:, None], i[None] <= i[:, None]))):
        cst[:, K_GF + 256 * d:K_GF + 256 * d + P] = strict
        cst[:, K_GF + 256 * d + P:K_GF + 256 * d + 256] = incl
    cst[:, K_SCAN:K_SCAN + SEQ] = np.arange(SEQ) % C != 0
    half = ROPE // 2
    cst[:, K_FREQ] = (np.float32(10000.0) ** (-np.arange(half, dtype=np.float32) / np.float32(half)))[i % half]
    for e in range(2):
        cst[:, K_HEAD + e], cst[:, K_NHEAD + e] = i // 64 == e, -0.5 * (i // 64 == e)
    cst[:, K_SIGN] = np.where(i % 64 < 32, -1, 1)
    cst[:, K_EPS], cst[:, K_GNEPS], cst[:, K_KKEPS] = EPS, GN_EPS, KK_EPS
    lev = np.zeros((P, len(LEVELS), 2, P), np.int32)
    for j, s in enumerate(LEVELS):
        low = ((i[:, None] // (2 * s) == i[None] // (2 * s)) & (i[:, None] % (2 * s) >= s) & (i[None] % (2 * s) < s))
        lev[:, j, 0], lev[:, j, 1] = low, low.T
    return cst, lev.reshape(P, -1)


def kernel(**inputs):
    import concourse.bacc as bacc
    from concourse.bass_utils import run_bass_kernel_spmd

    a = {k: np.asarray(v) for k, v in inputs.items()}
    cst, lev = _constants()
    cst[:, K_GAIN:K_GAIN + KD] = _columns(a["final_norm"])
    arrays = {"x_dram": np.ascontiguousarray(a["x"][0].T.reshape(KD, P, SEQ).transpose(1, 0, 2)),
              "c_dram": a["c"].reshape(1, DM), "pos_dram": a["positions"].reshape(1, SEQ),
              "cst_dram": cst, "lev_dram": lev}
    prm, tiles, mlp, ada, mlaw, lora = [], [], [], [], [], []
    base = 448
    for l in range(DEPTH):
        win = a["w_in"][l]
        kpe = np.concatenate([win[:, :384], win[:, 384:448], win[:, 384:448], win[:, base + 1536:]], axis=1)
        rkv = win[:, base:base + 1536]
        tiles.append(np.concatenate([_blocks(kpe, range(0, 896, P)),
                                     _blocks(rkv, [i * 512 + b * P for b in range(RB) for i in range(3)]),
                                     _blocks(a["w_out"][l], range(0, DM, P))]))
        wu = a["ffn_w_up"][l]
        g, v = _blocks(wu[:, :FF], range(0, FF, P)), _blocks(wu[:, FF:], range(0, FF, P))
        wd = a["ffn_w_down"][l].reshape(NDN, 2, P, KD, P).transpose(0, 2, 1, 3, 4)
        mlp.append(np.concatenate([np.stack([g, v], axis=2), wd]))
        ada.append(a["ada_w"][l].T.reshape(48, P, DM))
        uq = a["mla_w_uq"][l].reshape(2, P, HEADS, NOPE + ROPE)
        ukv = a["mla_w_ukv"][l].reshape(P, HEADS, NOPE + VD)
        pairs = []
        for hp in range(2):
            h0, h1 = 2 * hp, 2 * hp + 1
            q = np.concatenate([uq[:, :, h0, :NOPE], uq[:, :, h1, :NOPE], uq[:, :, h0, NOPE:], uq[:, :, h1, NOPE:]], axis=2)
            kv = np.concatenate([ukv[:, h0, :NOPE], ukv[:, h1, :NOPE], ukv[:, h0, NOPE:], ukv[:, h1, NOPE:]], axis=1)
            pairs.append(np.concatenate([q[0], q[1], kv], axis=1))
        mlaw.append(np.stack(pairs))
        w2, a2, g2 = a["rwkv_w2"][l].reshape(P, RW), a["rwkv_a2"][l].reshape(P, RW), a["rwkv_g2"][l]
        rows = (np.arange(P) < 64)[:, None]
        dirs = [np.where(rows, w2, 0), np.where(rows, 0, w2), np.where(rows, a2, 0), np.where(rows, 0, a2)]
        lora.append(np.stack([np.stack([m[:, b * P:(b + 1) * P] for m in (*dirs, g2)], axis=1) for b in range(RB)]))
        mu = a["rwkv_mu"][l]
        order = [1536, 1664, 1792] + [i * 512 + b * P for b in range(RB) for i in range(3)]
        mus = [np.stack([mu[j][s:s + P] for s in order], axis=1) for j in range(2)]
        prm.append(np.concatenate(
            [_columns(a["ada_b"][l]), _columns(a["mla_q_norm"][l]), _columns(a["mla_kv_norm"][l]),
             _columns(a["mla_out_norm"][l]), mus[0], mus[1], _columns(a["rwkv_w0"][l].reshape(-1)),
             _columns(a["rwkv_a0"][l].reshape(-1)), _columns(a["rwkv_k_k"][l]), _columns(a["rwkv_k_a"][l]),
             _columns(a["rwkv_r_k"][l].reshape(-1)), _columns(a["rwkv_gn_g"][l]), _columns(a["rwkv_gn_b"][l]),
             _columns(a["ffn_conv_w"][l].reshape(-1)), _columns(a["ffn_conv_b"][l])], axis=1))
    tiles.append(tiles[0][:3])
    arrays |= {"prm_dram": np.stack(prm), "tiles_dram": np.concatenate(tiles), "mlp_dram": np.concatenate(mlp),
               "ada_dram": np.stack(ada), "mlaw_dram": np.stack(mlaw),
               "lora_dram": np.stack(lora)}
    arrays = {k: np.ascontiguousarray(v) for k, v in arrays.items()}

    nc = bacc.Bacc("TRN2", target_bir_lowering=False, num_devices=1)
    aps = {n: nc.dram_tensor(n, v.shape, mybir.dt.from_np(v.dtype), kind="ExternalInput").ap() for n, v in arrays.items()}
    out = nc.dram_tensor("out_dram", (KD, P, SEQ), F32, kind="ExternalOutput").ap()
    names = ("x", "c", "pos", "cst", "lev", "prm", "tiles", "mlp", "ada", "mlaw", "lora")
    trunk(nc, *[aps[f"{n}_dram"] for n in names], out)
    r = run_bass_kernel_spmd(nc, [arrays], core_ids=[0])
    got = np.asarray(r.results[0]["out_dram"])
    return np.ascontiguousarray(got.transpose(2, 0, 1).reshape(1, SEQ, DM))
```
